# Optimizing a Trainium2 kernel written in Bass

```python
import math
import jax, jax.numpy as jnp
from jax import lax
import numpy as np

D_MODEL = 1024
BATCH = 1
SEQ = 256
DEPTH = 1
DEC_BATCH = 8
DEC_SEQ = 4
PAST_LEN = 2048
PAGE_SIZE = 128

D_MIX = D_MODEL
D_ATTN = D_MIX // 2
D_SSM = D_MIX - D_ATTN
HEAD_DIM = 64
N_HEADS = D_ATTN // HEAD_DIM
N_KV_HEADS = 2
GQA_GROUP = N_HEADS // N_KV_HEADS
WINDOW = 128
SSM_GROUP = 16
N_SSM_GROUPS = D_SSM // SSM_GROUP
SSM_STATE = 64
N_EXPERTS = 32
TOP_K = 4
D_FF = D_MODEL
SWIGLU_LIMIT = 7.0
SWIGLU_ALPHA = 1.702
MOE_BLOCK = 128
RMS_EPS = 1e-6
NEG_INF = -1e30
D_KV = N_KV_HEADS * HEAD_DIM
D_IN_PROJ = D_ATTN + 2 * D_KV + D_SSM

kernel_name = 'hymba_swa_sink_s5_moe_step'

def _rmsnorm(x, g):
    x32 = x.astype(jnp.float32)
    y = x32 * lax.rsqrt(jnp.mean(x32 * x32, axis=-1, keepdims=True) + RMS_EPS)
    return (y * g.astype(jnp.float32)).astype(x.dtype)

def _project(xn, w_in, q_norm_g, k_norm_g):
    b_, s_ = xn.shape[:2]
    h = xn @ w_in
    q, k, v, u = jnp.split(h, [D_ATTN, D_ATTN + D_KV, D_ATTN + 2 * D_KV], axis=-1)
    q = _rmsnorm(q.reshape(b_, s_, N_KV_HEADS, GQA_GROUP, HEAD_DIM), q_norm_g)
    k = _rmsnorm(k.reshape(b_, s_, N_KV_HEADS, HEAD_DIM), k_norm_g)
    v = v.reshape(b_, s_, N_KV_HEADS, HEAD_DIM)
    return q, k, v, u

def _sink_attention(q, k, v, mask, sinks):
    s = jnp.einsum('...qkgd,...jkd->...kgqj', q.astype(jnp.float32), k.astype(jnp.float32)) * (HEAD_DIM ** -0.5)
    s = jnp.where(mask, s, NEG_INF)
    sink = jnp.broadcast_to(sinks.astype(jnp.float32).reshape(N_KV_HEADS, GQA_GROUP, 1, 1), s.shape[:-1] + (1,))
    p = jax.nn.softmax(jnp.concatenate([s, sink], axis=-1), axis=-1)[..., :-1]
    return jnp.einsum('...kgqj,...jkd->...qkgd', p.astype(v.dtype), v)

def _band_attention(q, k, v, sinks):
    b_, s_ = q.shape[:2]
    nb = s_ // WINDOW
    qb = q.reshape(b_, nb, WINDOW, N_KV_HEADS, GQA_GROUP, HEAD_DIM)

    def with_prev(t):
        t = t.reshape(b_, nb, WINDOW, N_KV_HEADS, HEAD_DIM)
        prev = jnp.concatenate([jnp.zeros_like(t[:, :1]), t[:, :-1]], axis=1)
        return jnp.concatenate([prev, t], axis=2)

    kband, vband = with_prev(k), with_prev(v)
    blk = jnp.arange(nb)[:, None, None]
    qpos = blk * WINDOW + jnp.arange(WINDOW)[None, :, None]
    kpos = (blk - 1) * WINDOW + jnp.arange(2 * WINDOW)[None, None, :]
    mask = (kpos <= qpos) & (kpos > qpos - WINDOW) & (kpos >= 0)
    o = _sink_attention(qb, kband, vband, mask[:, None, None], sinks)
    return o.reshape(b_, s_, D_ATTN)

def _window_cache_attention(q, k, v, cache_k, cache_v, sinks):
    b_, n_new = q.shape[:2]
    n_buf = cache_k.shape[1]
    k_all = jnp.concatenate([cache_k.astype(k.dtype), k], axis=1)
    v_all = jnp.concatenate([cache_v.astype(v.dtype), v], axis=1)
    qpos = n_buf + jnp.arange(n_new)[:, None]
    kpos = jnp.arange(n_buf + n_new)[None, :]
    mask = (kpos <= qpos) & (kpos > qpos - WINDOW)
    o = _sink_attention(q, k_all, v_all, mask, sinks)
    return o.reshape(b_, n_new, D_ATTN), k_all[:, n_new:], v_all[:, n_new:]

def _s5(u, h0_re, h0_im, lam_re, lam_im, b_re, b_im, c_re, c_im, d_skip, log_dt):
    b_, s_ = u.shape[:2]
    u32 = u.astype(jnp.float32).reshape(b_, s_, N_SSM_GROUPS, SSM_GROUP)
    dt = jnp.exp(log_dt.astype(jnp.float32))[:, None]
    l_re = jnp.minimum(lam_re.astype(jnp.float32), -1e-4)
    l_im = lam_im.astype(jnp.float32)
    mag = jnp.exp(l_re * dt)
    a_re = mag * jnp.cos(l_im * dt)
    a_im = mag * jnp.sin(l_im * dt)
    den = l_re * l_re + l_im * l_im
    n_re = a_re - 1.0
    z_re = (n_re * l_re + a_im * l_im) / den
    z_im = (a_im * l_re - n_re * l_im) / den
    br, bi = b_re.astype(jnp.float32), b_im.astype(jnp.float32)
    bb_re = z_re[..., None] * br - z_im[..., None] * bi
    bb_im = z_re[..., None] * bi + z_im[..., None] * br
    bu_re = jnp.einsum('bsgh,gph->bsgp', u32, bb_re)
    bu_im = jnp.einsum('bsgh,gph->bsgp', u32, bb_im)
    h0r, h0i = h0_re.astype(jnp.float32), h0_im.astype(jnp.float32)
    bu_re = bu_re.at[:, 0].add(a_re * h0r - a_im * h0i)
    bu_im = bu_im.at[:, 0].add(a_re * h0i + a_im * h0r)
    ar = jnp.broadcast_to(a_re, bu_re.shape)
    ai = jnp.broadcast_to(a_im, bu_im.shape)

    def combine(e1, e2):
        a1r, a1i, b1r, b1i = e1
        a2r, a2i, b2r, b2i = e2
        return (a2r * a1r - a2i * a1i, a2r * a1i + a2i * a1r,
                a2r * b1r - a2i * b1i + b2r, a2r * b1i + a2i * b1r + b2i)

    _, _, h_re, h_im = lax.associative_scan(combine, (ar, ai, bu_re, bu_im), axis=1)
    y = (jnp.einsum('bsgp,ghp->bsgh', h_re, c_re.astype(jnp.float32))
         - jnp.einsum('bsgp,ghp->bsgh', h_im, c_im.astype(jnp.float32))
         + d_skip.astype(jnp.float32) * u32)
    return y.reshape(b_, s_, D_SSM), h_re[:, -1], h_im[:, -1]

def _glu(y, w_glu, b_glu):
    z = jax.nn.gelu(y) @ w_glu.astype(jnp.float32) + b_glu.astype(jnp.float32)
    a, g = jnp.split(z, 2, axis=-1)
    return a * jax.nn.sigmoid(g)

def _clamped_swiglu(h):
    x_glu = jnp.minimum(h[..., ::2], SWIGLU_LIMIT)
    x_lin = jnp.clip(h[..., 1::2], -SWIGLU_LIMIT, SWIGLU_LIMIT)
    return x_glu * jax.nn.sigmoid(SWIGLU_ALPHA * x_glu) * (x_lin + 1.0)

def _moe(x2d, w_router, b_router, w_gate_up, b_gate_up, w_down, b_down):
    t_ = x2d.shape[0]
    n_assign = t_ * TOP_K
    logits = x2d.astype(jnp.float32) @ w_router.astype(jnp.float32) + b_router.astype(jnp.float32)
    top_v, top_i = lax.top_k(logits, TOP_K)
    gates = jax.nn.softmax(top_v, axis=-1)
    flat_e = top_i.reshape(-1)
    flat_tok = jnp.arange(n_assign, dtype=jnp.int32) // TOP_K
    flat_w = gates.reshape(-1)
    order = jnp.argsort(flat_e)
    sorted_e = flat_e[order]
    counts = jnp.bincount(flat_e, length=N_EXPERTS)
    padded = ((counts + MOE_BLOCK - 1) // MOE_BLOCK) * MOE_BLOCK
    pend = jnp.cumsum(padded)
    pstart = pend - padded
    ustart = jnp.cumsum(counts) - counts
    dest = pstart[sorted_e] + (jnp.arange(n_assign) - ustart[sorted_e])
    n_rows = ((n_assign + MOE_BLOCK - 1) // MOE_BLOCK + N_EXPERTS) * MOE_BLOCK
    row_tok = jnp.zeros((n_rows,), jnp.int32).at[dest].set(flat_tok[order])
    row_w = jnp.zeros((n_rows,), jnp.float32).at[dest].set(flat_w[order])
    nb = n_rows // MOE_BLOCK
    block_start = jnp.arange(nb) * MOE_BLOCK
    block_e = jnp.minimum(jnp.sum(pend[None, :] <= block_start[:, None], axis=1), N_EXPERTS - 1)
    x_rows = x2d[row_tok].reshape(nb, MOE_BLOCK, x2d.shape[-1])

    def expert_block(args):
        xb, e = args
        h = xb @ w_gate_up[e] + b_gate_up[e]
        return _clamped_swiglu(h) @ w_down[e] + b_down[e]

    out = lax.map(expert_block, (x_rows, block_e)).reshape(n_rows, -1)
    y = jax.ops.segment_sum(out.astype(jnp.float32) * row_w[:, None], row_tok, num_segments=t_)
    return y.astype(x2d.dtype)

def _layer(x, lp, cache_k, cache_v, h0_re, h0_im):
    xn = _rmsnorm(x, lp['norm_mix_g'])
    q, k, v, u = _project(xn, lp['w_in'], lp['q_norm_g'], lp['k_norm_g'])
    if cache_k is None:
        attn = _band_attention(q, k, v, lp['attn_sinks'])
        new_k, new_v = k[:, -WINDOW:], v[:, -WINDOW:]
    else:
        attn, new_k, new_v = _window_cache_attention(q, k, v, cache_k, cache_v, lp['attn_sinks'])
    y_ssm, h_re, h_im = _s5(u, h0_re, h0_im, lp['ssm_lambda_re'], lp['ssm_lambda_im'], lp['ssm_b_re'],
                            lp['ssm_b_im'], lp['ssm_c_re'], lp['ssm_c_im'], lp['ssm_d'], lp['ssm_log_dt'])
    ssm_o = _glu(y_ssm, lp['w_glu'], lp['b_glu']).astype(x.dtype)
    merged = jnp.concatenate([_rmsnorm(attn.astype(x.dtype), lp['attn_out_norm_g']),
                              _rmsnorm(ssm_o, lp['ssm_out_norm_g'])], axis=-1)
    x = x + merged @ lp['w_out']
    xn2 = _rmsnorm(x, lp['norm_ffn_g'])
    y_ff = _moe(xn2.reshape(-1, D_MODEL), lp['w_router'], lp['b_router'], lp['w_gate_up'],
                lp['b_gate_up'], lp['w_down'], lp['b_down'])
    x = x + y_ff.reshape(x.shape)
    return x, new_k, new_v, h_re, h_im

def setup_inputs(seed: int = 0) -> dict:
    key = jax.random.key(seed)
    ks = jax.random.split(key, 40)
    f32 = jnp.float32
    win_rows = min(WINDOW, PAST_LEN)

    def nrm(k, shape, scale):
        return jax.random.normal(k, shape, f32) * scale

    def gain(k, width):
        return 1.0 + nrm(k, (DEPTH, width), 0.02)

    lam_im = jnp.broadcast_to(math.pi * jnp.arange(SSM_STATE, dtype=f32), (DEPTH, N_SSM_GROUPS, SSM_STATE))
    return {
        'x_prompt': nrm(ks[0], (BATCH, SEQ, D_MODEL), 1.0),
        'x_sample': nrm(ks[1], (DEC_BATCH, DEC_SEQ, D_MODEL), 1.0),
        'cache_k': nrm(ks[2], (DEPTH, DEC_BATCH, win_rows, N_KV_HEADS, HEAD_DIM), 1.0),
        'cache_v': nrm(ks[3], (DEPTH, DEC_BATCH, win_rows, N_KV_HEADS, HEAD_DIM), 1.0),
        'state_ssm_re': nrm(ks[4], (DEPTH, DEC_BATCH, N_SSM_GROUPS, SSM_STATE), 0.1),
        'state_ssm_im': nrm(ks[5], (DEPTH, DEC_BATCH, N_SSM_GROUPS, SSM_STATE), 0.1),
        'norm_mix_g': gain(ks[6], D_MODEL),
        'w_in': nrm(ks[7], (DEPTH, D_MODEL, D_IN_PROJ), D_MODEL ** -0.5),
        'q_norm_g': gain(ks[8], HEAD_DIM),
        'k_norm_g': gain(ks[9], HEAD_DIM),
        'attn_sinks': nrm(ks[10], (DEPTH, N_HEADS), 0.5),
        'ssm_lambda_re': -0.5 + nrm(ks[11], (DEPTH, N_SSM_GROUPS, SSM_STATE), 0.01),
        'ssm_lambda_im': lam_im + nrm(ks[12], (DEPTH, N_SSM_GROUPS, SSM_STATE), 0.01),
        'ssm_b_re': nrm(ks[13], (DEPTH, N_SSM_GROUPS, SSM_STATE, SSM_GROUP), (2 * SSM_GROUP) ** -0.5),
        'ssm_b_im': nrm(ks[14], (DEPTH, N_SSM_GROUPS, SSM_STATE, SSM_GROUP), (2 * SSM_GROUP) ** -0.5),
        'ssm_c_re': nrm(ks[15], (DEPTH, N_SSM_GROUPS, SSM_GROUP, SSM_STATE), (2 * SSM_STATE) ** -0.5),
        'ssm_c_im': nrm(ks[16], (DEPTH, N_SSM_GROUPS, SSM_GROUP, SSM_STATE), (2 * SSM_STATE) ** -0.5),
        'ssm_d': nrm(ks[17], (DEPTH, N_SSM_GROUPS, SSM_GROUP), 1.0),
        'ssm_log_dt': jax.random.uniform(ks[18], (DEPTH, N_SSM_GROUPS), f32, math.log(1e-3), math.log(1e-1)),
        'w_glu': nrm(ks[19], (DEPTH, D_SSM, 2 * D_SSM), D_SSM ** -0.5),
        'b_glu': nrm(ks[20], (DEPTH, 2 * D_SSM), 0.01),
        'attn_out_norm_g': gain(ks[21], D_ATTN),
        'ssm_out_norm_g': gain(ks[22], D_SSM),
        'w_out': nrm(ks[23], (DEPTH, D_MIX, D_MODEL), D_MIX ** -0.5),
        'norm_ffn_g': gain(ks[24], D_MODEL),
        'w_router': nrm(ks[25], (DEPTH, D_MODEL, N_EXPERTS), D_MODEL ** -0.5),
        'b_router': nrm(ks[26], (DEPTH, N_EXPERTS), 0.01),
        'w_gate_up': nrm(ks[27], (DEPTH, N_EXPERTS, D_MODEL, 2 * D_FF), D_MODEL ** -0.5),
        'b_gate_up': nrm(ks[28], (DEPTH, N_EXPERTS, 2 * D_FF), 0.01),
        'w_down': nrm(ks[29], (DEPTH, N_EXPERTS, D_FF, D_MODEL), D_FF ** -0.5),
        'b_down': nrm(ks[30], (DEPTH, N_EXPERTS, D_MODEL), 0.01),
    }

def reference(x_prompt, x_sample, cache_k, cache_v, state_ssm_re, state_ssm_im, norm_mix_g, w_in,
              q_norm_g, k_norm_g, attn_sinks, ssm_lambda_re, ssm_lambda_im, ssm_b_re, ssm_b_im,
              ssm_c_re, ssm_c_im, ssm_d, ssm_log_dt, w_glu, b_glu, attn_out_norm_g, ssm_out_norm_g,
              w_out, norm_ffn_g, w_router, b_router, w_gate_up, b_gate_up, w_down, b_down):
    xp, xs = x_prompt, x_sample
    kp_l, vp_l, rp_l, ip_l, ks_l, vs_l, rs_l, is_l = [], [], [], [], [], [], [], []
    h0 = jnp.zeros((xp.shape[0], N_SSM_GROUPS, SSM_STATE), jnp.float32)
    for layer in range(DEPTH):
        lp = dict(norm_mix_g=norm_mix_g[layer], w_in=w_in[layer], q_norm_g=q_norm_g[layer],
                  k_norm_g=k_norm_g[layer], attn_sinks=attn_sinks[layer],
                  ssm_lambda_re=ssm_lambda_re[layer], ssm_lambda_im=ssm_lambda_im[layer],
                  ssm_b_re=ssm_b_re[layer], ssm_b_im=ssm_b_im[layer], ssm_c_re=ssm_c_re[layer],
                  ssm_c_im=ssm_c_im[layer], ssm_d=ssm_d[layer], ssm_log_dt=ssm_log_dt[layer],
                  w_glu=w_glu[layer], b_glu=b_glu[layer], attn_out_norm_g=attn_out_norm_g[layer],
                  ssm_out_norm_g=ssm_out_norm_g[layer], w_out=w_out[layer], norm_ffn_g=norm_ffn_g[layer],
                  w_router=w_router[layer], b_router=b_router[layer], w_gate_up=w_gate_up[layer],
                  b_gate_up=b_gate_up[layer], w_down=w_down[layer], b_down=b_down[layer])
        xp, kp, vp, rp, ip = _layer(xp, lp, None, None, h0, h0)
        xs, ksn, vsn, rsn, isn = _layer(xs, lp, cache_k[layer], cache_v[layer],
                                        state_ssm_re[layer], state_ssm_im[layer])
        kp_l.append(kp); vp_l.append(vp); rp_l.append(rp); ip_l.append(ip)
        ks_l.append(ksn); vs_l.append(vsn); rs_l.append(rsn); is_l.append(isn)
    new_k_prompt, new_v_prompt = jnp.stack(kp_l), jnp.stack(vp_l)
    new_ssm_re_prompt, new_ssm_im_prompt = jnp.stack(rp_l), jnp.stack(ip_l)
    new_k_sample, new_v_sample = jnp.stack(ks_l), jnp.stack(vs_l)
    new_ssm_re_sample, new_ssm_im_sample = jnp.stack(rs_l), jnp.stack(is_l)
    return (xp, xs, new_k_prompt, new_v_prompt, new_ssm_re_prompt, new_ssm_im_prompt,
            new_k_sample, new_v_sample, new_ssm_re_sample, new_ssm_im_sample)


_drawn_inputs = setup_inputs


def setup_inputs(seed=0):
    import zlib

    import numpy as np

    out = dict(_drawn_inputs(seed))
    spreads = {}
    factors = {'ssm_lambda_re': 18.973, 'b_gate_up': 8.0, 'b_down': 8.0, 'attn_sinks': 7.233}
    for name, (base, spread) in spreads.items():
        noise = np.random.default_rng([zlib.crc32(name.encode()), seed]).standard_normal(out[name].shape)
        drawn = base * np.exp(spread * noise) if base else spread * noise
        out[name] = __import__('jax').numpy.asarray(drawn.astype(out[name].dtype))
    for name, factor in factors.items():
        out[name] = (out[name] * factor).astype(out[name].dtype)
    return out
```

```python
import numpy as np

import concourse.bass as bass
from concourse import mybir

F32 = mybir.dt.float32
I32 = mybir.dt.int32
U32 = mybir.dt.uint32
ALU = mybir.AluOpType
ACT = mybir.ActivationFunctionType
AX = mybir.AxisListType

P = 128
D = 1024
KT = D // P
NP, NB, NS = 256, 8, 4
NSAMP = NB * NS
T = NP + NSAMP
WIN = 128
DS = 512
CT = DS // P
HD = 64
NG, SG, SS = 32, 16, 64
ST = NG * SS // P
NE, TOPK = 32, 4
SLOTS = 64
ROUNDS = -(-T // SLOTS)
PAIRS = NE // 2
EPS = 1e-6
NEG = -1e30
TT = ((0, P), (P, P), (2 * P, T - 2 * P))
NPAR = ST + CT * SS
SAMPLE_KEYS = NB * WIN + NSAMP
TWO_PI = 2 * np.pi
TWO_PI_HI = 6.28125
TWO_PI_LO = float(np.float32(TWO_PI - TWO_PI_HI))
ROUND_MAGIC = 1.5 * 2.0 ** 23
GELU_C = float(np.sqrt(2 / np.pi))

C_GMIX, C_GFFN, C_GQ, C_GK, C_GATT, C_GSSM, C_BA, C_BG, C_D, C_SINK, C_BR = np.cumsum(
    [0, 8, 8, 1, 1, 4, 4, 4, 4, 4, 10]).tolist()
N_COLS = C_BR + NE


def build(nc, a):
    base = nc.sbuf_base
    base += -base % 32
    marks = {"at": base}

    def sb(name, shape, at, dt=F32):
        t = nc.alloc_sbuf_tensor_at(name, [P] + list(shape), dt, offset=base + at)
        return t

    def sz(*shape):
        return int(np.prod(shape)) * 4

    GU, DN = 0, 65536
    REST = 131072
    gu_ring = [sb(f"gu_ring{k}", [2 * D], GU + k * 8192) for k in range(8)]
    dn_ring = [sb(f"dn_ring{k}", [2, D], DN + k * 8192) for k in range(8)]
    w_in = sb("w_in", [10, KT, P], GU)
    pT = sb("pT", [42 * P], GU)
    s_p0 = sb("s_p0", [8, P], GU + 21504)
    s_p1 = sb("s_p1", [8, 2 * P], GU + 25600)
    yT = sb("yT", [CT, T], GU + 33792)
    s_s = sb("s_s", [2, SAMPLE_KEYS], GU + 40960)
    kT = sb("kT", [T], GU + 49408)
    vT = sb("vT", [T], GU + 50560)
    v_tok = sb("v_tok", [3, P], GU + 51712)
    q_rot = [sb(f"q_rot{b}", [2, 2, T], GU + 53248 + b * 4608) for b in range(2)]
    q_s = sb("q_s", [CT * NSAMP], GU + 62464)
    tab_tmp_p = sb("tab_tmp_p", [2, 2, 256], GU + 53248)
    cs = sb("cs", [ST, 2, T], DN)
    w_glu = sb("w_glu", [CT, D], DN + 36864)
    cacheK = sb("cacheK", [NB, WIN], DN + 53248)
    cacheV = sb("cacheV", [NB, P], DN + 57344)
    b_bar = sb("b_bar", [2, CT, P], DN + 61440)
    o = REST
    xT = sb("xT", [KT, T], o); o += 9216
    xg = sb("xg", [KT, T], o)
    mask_p = sb("mask_p", [2 * P], o)
    mask_s = sb("mask_s", [SAMPLE_KEYS], o + 1024); o += 9216
    W16 = o; o += 16384
    w_out = sb("w_out", [CT, D], W16)
    QQ = o
    qT = sb("qT", [CT, T], o); o += 4608
    aT = sb("aT", [CT, T], o)
    ms = sb("ms", [T], o)
    r_mix = sb("r_mix", [T], o + 1152)
    qsq = sb("qsq", [T], o + 2304)
    vv = sb("vv", [T], o + 3456); o += 4608
    xsq = sb("xsq", [KT, T], QQ)
    uT = sb("uT", [CT, T], o); o += 4608
    WK = o
    p1 = sb("p1", [2, T], o); p2 = sb("p2", [2, T], o + 2304)
    v_rot = sb("v_rot", [2, T], o + 4608)
    g_rot = [sb(f"g_rot{b}", [2, T], o + 6912 + b * 2304) for b in range(2)]
    r_scan = [sb(f"r_scan{b}", [2, T], o + 11520 + b * 2304) for b in range(2)]
    b_raw = sb("b_raw", [2, CT, P], WK)
    e_tab = sb("e_tab", [2, ST, 16], GU + 40960)
    f_tab = sb("f_tab", [2, ST, 16], GU + 43008)
    t1 = sb("t1", [2, ST, 16], WK + 8192)
    t2 = sb("t2", [2, ST, 16], WK + 10240)
    tab_tmp = sb("tab_tmp", [2, 2, 256], WK + 8192)
    o += 16128
    ident = sb("ident", [P], o); o += 512
    ones = sb("ones", [P], o); o += 512
    block_ones = sb("block_ones", [P], o); o += 512
    tri = sb("tri", [P], o); o += 512
    scan_pat = sb("scan_pat", [T], o); o += 1152
    iota = sb("iota", [SLOTS], o); o += 256
    cT = sb("cT", [3, ST, 32], o); o += 6144
    cols = sb("cols", [N_COLS], o); o += 352
    h0 = sb("h0", [ST, 2, NB], o); o += 1024
    h_last = sb("h_last", [ST, 2, NB + 1], o); o += 1152
    st_mx = sb("st_mx", [24], o); st_neg = sb("st_neg", [18], o + 96)
    st_sum = sb("st_sum", [18], o + 192); st_snk = sb("st_snk", [18], o + 288); o += 384
    mag = sb("mag", [ST], o); o += 64
    flag = sb("flag", [8], o, I32); o += 32
    assert base + o <= nc.sbuf_usable_end, (base + o, nc.sbuf_usable_end)
    par = sb("par", [3, NPAR], W16)
    par_t = [sb(f"par_t{k}", [NPAR], W16 + 3 * sz(NPAR) + k * sz(NPAR)) for k in range(11)]
    bb_tmp = sb("bb_tmp", [2, CT, P], GU + 57344)
    o = W16
    x_tok = [sb(f"x_tok{t}", [D], o + 4096 * t) for t in range(3)]; o += 12288
    xe = sb("xe", [KT, P], o); o += 4096
    ye_T = sb("ye_T", [KT, 2, SLOTS], o); o += 4096
    YE = o
    ye = sb("ye", [D], o); o += 4096
    hg = sb("hg", [KT, SLOTS], o); o += 2048
    hl = sb("hl", [KT, SLOTS], o); o += 2048
    th = sb("th", [KT, SLOTS], o); o += 2048
    hT = sb("hT", [KT, SLOTS], o); o += 2048
    b_gu = sb("b_gu", [NE * 16], o); o += 2048
    b_dn = sb("b_dn", [NE * 8], o); o += 1024
    oh = sb("oh", [3, P], o); o += 1536
    goh = sb("goh", [3, P], o); o += 1536
    gT = sb("gT", [T], o); o += 1152
    pos = sb("pos", [3, NE + 4], o); o += 448
    gate = sb("gate", [3, NE + 4], o); o += 448
    sel = sb("sel", [3, NE], o); o += 384
    lg = sb("lg", [3, NE], o); o += 384
    v8 = sb("v8", [3, 8], o); o += 96
    i8 = sb("i8", [3, 8], o, U32); o += 96
    if8 = sb("if8", [3, 8], o); o += 96
    ex4 = sb("ex4", [3, 4], o); o += 64
    gs = sb("gs", [3], o); o += 32
    eq = sb("eq", [3, NE], o); o += 384
    w_r = sb("w_r", [KT, NE], o); o += 1024
    x2sq = sb("x2sq", [2, T], YE)
    r2 = sb("r2", [T], YE + 2304)
    cnt = sb("cnt", [8], o); o += 32
    assert o <= WK + 16128, (o, WK + 16128)

    pb = [nc.alloc_psum_tensor(f"bank{k}", [P, 512], F32) for k in range(8)]
    sems = {}

    def S(name):
        if name not in sems:
            sems[name] = nc.alloc_semaphore(name)
        return sems[name]

    x_in = [S(f"x_in{h}") for h in range(2)]
    wu_in = [S(f"wu_in{c}") for c in range(CT)]
    wq_in = [S(f"wq_in{c}") for c in range(3)]
    for n in ("par_in cols_in b_in const_in c_in h0_in mask_in cacheK_in cacheV_in wglu_in woutA_in woutB_in moe_in "
              "wr_in out_done "
              "xsq_ready xg_ready sum_ready ms_ready ln_done r_mix_ready u_proj u_ready proj_done proj_free "
              "sq_ready qk_sum vv_ready rq_ready raw_ready qk_ready v_ready v_turned v_tok_ready "
              "par_dve par_act bbar_ready bbar_step tab_dve tab_pool tab_act r_scan_ready w_ready w_free g_ready "
              "rot_ready rot_used y_sum y_ready ysq_ready y_poly tanh_ready gelu_ready h0_scaled hlast_step c_neg "
              "score_ready score_used neg_ready exp_done sum_inv p_ready pt_turned pt_ready pv_ready a_part_ready "
              "asq_ready asum_ready qs_ready av_ready ar_ready an_ready outA_done xmid_ready "
              "glu_done ga_ready th_glu s_ready ssq_ready ssum_ready sv_ready sr_ready sn_ready outB_done x2_ready "
              "x2sq_ready x2sum_ready x2v_ready r2_ready xn_ready logits_ready xtok_turned xtok_ready top_ready "
              "exp4_done sel_ready pos_ready route_ready yt_zeroed "
              "oh_ready gathered xe_ready gu_used gu_free hg_ready th_ready h_ready dn_used y_done "
              "goh_ready g_turned gT_ready y_turned ye_ready comb_done acc_done "
              "den_ready den_inv hl_ready hlg_ready goh_step pos_moved h_out "
              "dve_order act_order pool_order result_ready").split():
        S(n)
    gu_in = [S(f"gu_in{k}") for k in range(8)]
    dn_in = [S(f"dn_in{k}") for k in range(8)]
    order = {"dve": 0, "act": 0, "pool": 0}

    def ordered(eng, who, ins):
        order[who] += 1
        ins.then_inc(S(who + "_order"), 1)
        eng.wait_ge(S(who + "_order"), order[who])

    def col(k, n=P):
        return cols[0:n, k:k + 1]

    def wide(ap, axis, n):
        shape = list(ap.shape)
        return ap.unsqueeze(axis).to_broadcast(shape[:axis] + [n] + shape[axis:])

    SCORES = [("p0", 0, 0), ("p0", 1, 0), ("p1", 0, 0), ("p1", 0, 1), ("p1", 1, 0), ("p1", 1, 1),
              ("s", 0, 0), ("s", 0, 1), ("n", 0, 0), ("s", 1, 0), ("s", 1, 1), ("n", 1, 0)]
    TURNS = [("p0", 0, 0), ("p0", 1, 0), ("p1", 0, 0), ("p1", 0, 1), ("p1", 1, 0), ("p1", 1, 1),
             ("s", 0, 0), ("s", 0, 1), ("n", 0, 0), ("s", 1, 0), ("s", 1, 1), ("n", 1, 0)]
    PT_AT, at = [], 0
    for kind, _, _ in TURNS:
        PT_AT.append(at)
        at += 1 if kind == "n" else 4
    assert at == 42
    SCORE_SLOT = {0: range(0, 3), 1: range(3, 6), 2: range(6, 9), 3: range(9, 12)}
    TURN_SLOT = {6: range(0, 4), 7: range(4, 8), 8: range(8, 12)}
    PV_SLOT = 9
    ASUM_SLOT = 10
    OUTA_SLOT = {12: range(0, 2), 13: range(2, 4), 14: range(4, 6), 15: range(6, 8)}
    SLOTS_N = ST + 2

    def load_gu(sp, e, k):
        sp.dma_start(gu_ring[k][:], a["w_gu"][e, k]).then_inc(gu_in[k], 16)

    def load_dn(sp, e, c, j):
        k = 4 * j + c
        sp.dma_start(dn_ring[k][:], a["w_dn"][e, c]).then_inc(dn_in[k], 16)

    def load_expert0(sp, r, wait=False):
        if wait:
            sp.wait_ge(S("gu_used"), r * (8 * NE))
        for k in range(8):
            load_gu(sp, 0, k)
        if wait:
            sp.wait_ge(S("dn_used"), r * (4 * NE))
        for j in range(2):
            for c in range(4):
                load_dn(sp, j, c, j)

    def loads_of_round(sp, r):
        def gu(e, e_before, k):
            sp.wait_ge(S("gu_used"), e_before * 8 + (r * (8 * NE) + k + 1))
            load_gu(sp, e, k)

        with sp.Fori(0, PAIRS - 1) as i:
            for k in range(8):
                gu(i * 2 + 1, i * 2, k)
            for c in range(4):
                sp.wait_ge(S("dn_used"), i * 8 + (r * (4 * NE) + c + 1))
                load_dn(sp, i * 2 + 2, c, 0)
            for k in range(8):
                gu(i * 2 + 2, i * 2 + 1, k)
            for c in range(4):
                sp.wait_ge(S("dn_used"), i * 8 + (r * (4 * NE) + 4 + c + 1))
                load_dn(sp, i * 2 + 3, c, 1)
        for k in range(8):
            gu(NE - 1, NE - 2, k)

    def pT_sq(c):
        return pT[:, c * T:(c + 1) * T]

    def vsq(c):
        return (p1, p2)[c // 2][:, c % 2]

    def v_glu(x, c):
        return g_rot[c % 2][:, x]

    def gelu_tmp(c):
        return qT[:, c]

    def gelu_square(act, c):
        act.wait_ge(S("y_ready"), c + 1)
        nc.scalar.activation(gelu_tmp(c), yT[:, c], ACT.Square).then_inc(S("ysq_ready"), 1)

    def gelu_tanh(act, c):
        act.wait_ge(S("y_poly"), c + 1)
        nc.scalar.activation(gelu_tmp(c), gelu_tmp(c), ACT.Tanh, scale=GELU_C).then_inc(S("tanh_ready"), 1)

    def table(eng, e, t, tmp, who):
        o1 = tmp[:, 0].rearrange("p x (a b) -> p x a b", a=16)
        o2 = tmp[:, 1].rearrange("p x (a b) -> p x a b", a=16)
        src = wide(e_tab[:, :, t, :], 2, 16)
        eng.tensor_tensor(o1, src, wide(wide(f_tab[:, 0, t, :], 1, 2), 3, 16), ALU.mult)
        ordered(e, who, eng.tensor_tensor(o2, src, wide(wide(f_tab[:, 1, t, :], 1, 2), 3, 16), ALU.mult))
        eng.tensor_tensor(cs[:, t, 0, 0:NP], tmp[:, 0, 0], tmp[:, 1, 1], ALU.subtract)
        return eng.tensor_tensor(cs[:, t, 1, 0:NP], tmp[:, 0, 1], tmp[:, 1, 0], ALU.add)

    block = nc.Block()
    block.__enter__()

    @block.sync
    def _(sp):
        for h in range(2):
            sp.dma_start(xT[:, 4 * h:4 * h + 4, :], a["xT"][:, 4 * h:4 * h + 4, :]).then_inc(x_in[h], 16)
        for c in range(CT):
            sp.dma_start(w_in[:, c], a["w_in"][:, c]).then_inc(wu_in[c], 16)
        for c in range(3):
            sp.dma_start(w_in[:, 4 + 2 * c:6 + 2 * c], a["w_in"][:, 4 + 2 * c:6 + 2 * c]).then_inc(wq_in[c], 16)
        sp.dma_start(cacheK[:], a["cacheK"]).then_inc(S("cacheK_in"), 16)
        sp.dma_start(cacheV[:], a["cacheV"]).then_inc(S("cacheV_in"), 16)
        sp.dma_start(w_glu[:], a["w_glu"]).then_inc(S("wglu_in"), 16)
        sp.wait_ge(S("proj_done"), 6)
        sp.dma_start(mask_p[:], a["mask_p"]).then_inc(S("mask_in"), 16)
        sp.dma_start(mask_s[:], a["mask_s"]).then_inc(S("mask_in"), 16)
        sp.wait_ge(S("bbar_ready"), 1)
        sp.wait_ge(S("h0_scaled"), 1)
        sp.dma_start(w_out[:], a["w_out"][:, 0:CT]).then_inc(S("woutA_in"), 16)
        sp.wait_ge(S("qk_ready"), 5)
        sp.wait_ge(S("v_tok_ready"), 3)
        sp.wait_ge(S("v_ready"), 1)
        sp.dma_start(a["new_k"][:], kT[:, P:T]).then_inc(S("out_done"), 16)
        sp.dma_start(a["new_v"][:], vT[:, P:T]).then_inc(S("out_done"), 16)
        sp.wait_ge(S("cacheK_in"), 16)
        sp.wait_ge(S("cacheV_in"), 16)
        sp.dma_start(a["roll_k"][:], cacheK[:, :, NS:WIN]).then_inc(S("out_done"), 16)
        sp.dma_start(a["roll_v"][:], cacheV[NS:WIN]).then_inc(S("out_done"), 16)
        sp.wait_ge(S("outA_done"), KT)
        sp.dma_start(w_out[:], a["w_out"][:, CT:2 * CT]).then_inc(S("woutB_in"), 16)
        sp.wait_ge(S("glu_done"), 8)
        sp.wait_ge(S("out_done"), 64)
        sp.wait_ge(S("hlast_step"), 2 * ST)
        load_expert0(sp, 0)
        sp.wait_ge(S("sn_ready"), CT)
        sp.dma_start(w_r[:], a["w_r"]).then_inc(S("wr_in"), 16)
        sp.dma_start(b_gu[:], a["b_gu"]).then_inc(S("moe_in"), 16)
        sp.dma_start(b_dn[:], a["b_dn"]).then_inc(S("moe_in"), 16)
        loads_of_round(sp, 0)
        sp.wait_ge(S("route_ready"), 1)
        n = sp.alloc_register("sp_max_count")
        sp.reg_load(n, flag[0:1, 0:1])
        with sp.If_cmp(n, SLOTS, "IS_GT"):
            with sp.Fori(1, ROUNDS) as r:
                load_expert0(sp, r, True)
                loads_of_round(sp, r)
        sp.wait_ge(S("result_ready"), 1)
        sp.dma_start(a["y"][:], xT[:]).then_inc(S("out_done"), 16)
        sp.wait_ge(S("out_done"), 16 * 5)

    @block.tensor
    def _(pe):
        def mm(out, lhsT, rhs, start, stop, **kw):
            return nc.tensor.matmul(out, lhsT, rhs, start=start, stop=stop, **kw)

        pe.wait_ge(S("const_in"), 96)
        for k in range(KT):
            pe.wait_ge(S("xsq_ready"), k + 1)
            last = mm(pb[4][:, 0:T], ones[:], xsq[:, k], k == 0, k == KT - 1)
        last.then_inc(S("sum_ready"), 1)
        pe.wait_ge(S("xg_ready"), KT)
        for c in range(CT):
            pe.wait_ge(wu_in[c], 16)
            for k in range(KT):
                last = mm(pb[c][:, 0:T], w_in[:, c, k], xg[:, k], k == 0, k == KT - 1)
            last.then_inc(S("u_proj"), 1)

        def head_sums(i):
            pe.wait_ge(S("sq_ready"), i + 1)
            if i:
                pe.wait_ge(S("vv_ready"), i)
            mm(pb[7][:, 0:T], block_ones[:], qsq[:], True, True).then_inc(S("qk_sum"), 1)

        for i in range(6):
            pe.wait_ge(wq_in[i // 2], 16)
            if i >= 2:
                pe.wait_ge(S("proj_free"), i - 1)
            for k in range(KT):
                last = mm(pb[5 + i % 2][:, 0:T], w_in[:, 4 + i, k], xg[:, k], k == 0, k == KT - 1)
            last.then_inc(S("proj_done"), 1)
            if i:
                head_sums(i - 1)
        pe.wait_ge(S("v_ready"), 1)
        pe.wait_ge(S("vv_ready"), 5)
        for t, (f, n) in enumerate(TT):
            pe.transpose(pb[7][0:n, t * P:(t + 1) * P], vT[:, f:f + n], ident[:]).then_inc(S("v_turned"), 1)

        def input_product(t):
            c, j = t // 4, t % 4
            if t == 0:
                pe.wait_ge(S("bbar_ready"), 1)
                pe.wait_ge(S("u_ready"), CT)
            if t >= 2:
                pe.wait_ge(S("w_free"), t - 1)
            b = 2 * (t % 2)
            rows = slice(32 * j, 32 * j + 32)
            for x in range(2):
                last = mm(pb[b + x][:, 0:T], b_bar[rows, x, c], uT[rows, c], True, True)
            last.then_inc(S("w_ready"), 1)

        def output_product(t):
            c, j = t // 4, t % 4
            pe.wait_ge(S("rot_ready"), 2 * t + 2)
            if t == 0:
                pe.wait_ge(S("v_tok_ready"), 3)
                pe.wait_ge(S("c_neg"), 2)
            if c >= 2 and j == 0:
                pe.wait_ge(S("y_ready"), c - 1)
            out = pb[4 + 3 * (c % 2)][32 * j:32 * j + 32, 0:T]
            q = q_rot[t % 2]
            for n, (m, x) in enumerate(((0, q[:, 0, 0]), (1, q[:, 1, 1]), (2, q[:, 1, 0]), (2, q[:, 0, 1]))):
                last = mm(out, cT[:, m, t], x, n == 0, n == 3, tile_position=(0, 32 * j))
            last.then_inc(S("rot_used"), 1)

        def score(n):
            kind, kv, part = SCORES[n]
            bank = pb[5 + n % 2]
            if n >= 2:
                pe.wait_ge(S("score_used"), n - 1)
            else:
                pe.wait_ge(S("qk_ready"), 5)
                pe.wait_ge(S("v_ready"), 1)
            rows = slice(HD * kv, HD * kv + HD)
            if kind == "p0":
                for i in range(4):
                    last = mm(bank[:, i * P:(i + 1) * P], qT[rows, i, 0:P], kT[rows, 0:P], True, True)
            elif kind == "p1":
                for i in range(2):
                    last = mm(bank[:, i * 2 * P:(i + 1) * 2 * P], qT[rows, 2 * part + i, P:2 * P], kT[rows, 0:2 * P],
                              True, True)
            elif kind == "s":
                pe.wait_ge(S("qs_ready"), 1)
                pe.wait_ge(S("cacheK_in"), 16)
                last = mm(bank[:], q_s[rows], cacheK[rows, 4 * part:4 * part + 4, :], True, True)
            else:
                last = mm(bank[:, 0:NSAMP], q_s[rows], kT[rows, NP:T], True, True)
            last.then_inc(S("score_ready"), 1)

        def turn(n):
            kind, kv, part = TURNS[n]
            bank = pb[5 + n % 2]
            if n < 2:
                pe.wait_ge(S("score_used"), 12)
            else:
                pe.wait_ge(S("pt_ready"), n - 1)
            pe.wait_ge(S("p_ready"), {"p0": 1, "p1": 2, "s": 3 + kv, "n": 3 + kv}[kind])
            for i in range(1 if kind == "n" else 4):
                if kind == "p0":
                    src = s_p0[:, 4 * kv + i]
                elif kind == "p1":
                    src = s_p1[:, 4 * kv + i, part * P:(part + 1) * P]
                elif kind == "s":
                    src = s_s[:, kv, (4 * part + i) * WIN:(4 * part + i + 1) * WIN]
                else:
                    src = s_s[:, kv, NB * WIN:]
                m = src.shape[1]
                last = pe.transpose(bank[0:m, i * P:(i + 1) * P], src, ident[:])
            last.then_inc(S("pt_turned"), 1)

        def values(n):
            bank = pb[5 + n % 2]
            pe.wait_ge(S("pt_ready"), 12)
            if n == 2:
                pe.wait_ge(S("a_part_ready"), 1)
            for kv in range(2):
                out = bank[HD * kv:HD * kv + HD, :]
                d = slice(HD * kv, HD * kv + HD)
                at = [PT_AT[k] * P for k, u in enumerate(TURNS) if u[1] == kv]
                if n == 0:
                    last = mm(out, v_tok[:, 0, d], pT[:, at[0]:at[0] + 512], True, True, tile_position=(0, HD * kv))
                elif n == 1:
                    for b in range(2):
                        last = mm(out, v_tok[:, b, d], pT[:, at[1 + b]:at[1 + b] + 512], b == 0, b == 1,
                                  tile_position=(0, HD * kv))
                else:
                    pe.wait_ge(S("cacheV_in"), 16)
                    for b in range(NB):
                        f = at[3 + b // 4] + (b % 4) * P
                        mm(out[:, 0:P], cacheV[:, b, d], pT[:, f:f + P], b == 0, False, tile_position=(0, HD * kv))
                    last = mm(out[:, 0:P], v_tok[0:NSAMP, 2, d], pT[0:NSAMP, at[5]:at[5] + P], False, True,
                              tile_position=(0, HD * kv))
            last.then_inc(S("pv_ready"), 1)

        def square_sum(bank, sq, ready, signal):
            for c in range(CT):
                pe.wait_ge(S(ready), c + 1)
                last = mm(pb[bank][:, 0:T], ones[:], sq[c], c == 0, c == CT - 1)
            last.then_inc(S(signal), 1)

        for t in range(SLOTS_N):
            if t < ST:
                input_product(t)
            for n in SCORE_SLOT.get(t, ()):
                score(n)
            for n in TURN_SLOT.get(t, ()):
                turn(n)
            if t == PV_SLOT:
                for n in range(3):
                    values(n)
            if t == ASUM_SLOT:
                pe.wait_ge(S("a_part_ready"), 2)
                square_sum(6, [pT_sq(c) for c in range(CT)], "asq_ready", "asum_ready")
            for m in OUTA_SLOT.get(t, ()):
                if m == 0:
                    pe.wait_ge(S("woutA_in"), 16)
                    pe.wait_ge(S("an_ready"), CT)
                    pe.wait_ge(S("a_part_ready"), 3)
                if m >= 2:
                    pe.wait_ge(S("xmid_ready"), m - 1)
                for k in range(CT):
                    last = mm(pb[5 + m % 2][:, 0:T], w_out[:, k, m * P:(m + 1) * P], aT[:, k], k == 0, k == CT - 1)
                last.then_inc(S("outA_done"), 1)
            if t >= 2:
                output_product(t - 2)
        pe.wait_ge(S("wglu_in"), 16)
        for n in range(2 * CT):
            m = n // 2 + CT * (n % 2)
            if n < 4:
                pe.wait_ge(S("w_free"), ST)
            else:
                pe.wait_ge(S("ga_ready" if n % 2 == 0 else "th_glu"), n // 2 - 1)
            for k in range(CT):
                if n == 0:
                    pe.wait_ge(S("gelu_ready"), k + 1)
                last = mm(pb[n % 4][:, 0:T], w_glu[:, k, m * P:(m + 1) * P], yT[:, k], k == 0, k == CT - 1)
            last.then_inc(S("glu_done"), 1)
        pe.wait_ge(S("y_ready"), CT)
        square_sum(4, [vsq(c) for c in range(CT)], "ssq_ready", "ssum_ready")
        pe.wait_ge(S("sn_ready"), CT)
        pe.wait_ge(S("woutB_in"), 16)
        for m in range(KT):
            if m >= 4:
                pe.wait_ge(S("x2_ready"), m - 3)
            for k in range(CT):
                last = mm(pb[m % 4][:, 0:T], w_out[:, k, m * P:(m + 1) * P], uT[:, k], k == 0, k == CT - 1)
            last.then_inc(S("outB_done"), 1)
        pe.wait_ge(S("sv_ready"), 1)
        for k in range(KT):
            pe.wait_ge(S("x2sq_ready"), k + 1)
            mm(pb[4][:, 0:T], ones[:], x2sq[:, k % 2], k == 0, k == KT - 1).then_inc(S("x2sum_ready"), 1)
        pe.wait_ge(S("wr_in"), 16)
        pe.wait_ge(S("xn_ready"), KT)
        for t, (f, n) in enumerate(TT):
            for k in range(KT):
                last = mm(pb[5][0:n, t * NE:(t + 1) * NE], xg[:, k, f:f + n], w_r[:, k], k == 0, k == KT - 1)
            last.then_inc(S("logits_ready"), 1)
        for u in range(6):
            t, half = u // 2, u % 2
            f, n = TT[t]
            if u == 0:
                pe.wait_ge(S("x2_ready"), KT)
            for k in range(4):
                last = pe.transpose(pb[(0, 1, 2, 3, 6, 7)[u]][0:n, k * P:(k + 1) * P], xg[:, 4 * half + k, f:f + n],
                                    ident[:])
            last.then_inc(S("xtok_turned"), 1)
        pe.wait_ge(S("sel_ready"), 1)
        pe.wait_ge(S("x2v_ready"), 1)
        for t in range(3):
            for s in range(t + 1):
                mm(pb[4][:, t * NE:(t + 1) * NE], ones[:] if s < t else tri[:], sel[:, s], s == 0, s == t)
        for s in range(3):
            last = mm(pb[4][:, 3 * NE:4 * NE], ones[:], sel[:, s], s == 0, s == 2)
        last.then_inc(S("pos_ready"), 1)
        pe.wait_ge(S("xtok_ready"), 6)

        def gather(g):
            pe.wait_ge(S("oh_ready"), g + 1)
            for k in range(KT):
                out = pb[3 + k // 4][:, (k % 4) * P:(k % 4 + 1) * P]
                for t, (f, n) in enumerate(TT):
                    last = mm(out, x_tok[t][0:n, k * P:(k + 1) * P], oh[0:n, t], t == 0, t == 2)
                if k % 4 == 3:
                    last.then_inc(S("gathered"), 1)

        def gate_up(n, j):
            pe.wait_ge(S("xe_ready"), n["g"] * 2 + 2)
            pe.wait_ge(S("gu_free"), n["e2"] + j)
            for k in range(8):
                pe.wait_ge(gu_in[k], n["n"] * 32 + 16 * (j + 1))
                for m in range(16):
                    last = mm(pb[m // 8][:, (m % 8) * SLOTS:(m % 8 + 1) * SLOTS], gu_ring[k][:, m * P:(m + 1) * P],
                              xe[:, k, j * SLOTS:(j + 1) * SLOTS], k == 0 and m % 8 == 0, k == 7,
                              skip_group_check=True)
                last.then_inc(S("gu_used"), 1)

        def down(n, j):
            pe.wait_ge(S("h_ready"), n["e2"] + j)
            pe.wait_ge(S("y_done"), n["e2"] + j)
            for c in range(4):
                pe.wait_ge(dn_in[4 * j + c], n["n"] * 16 + 16)
                for kk in range(2):
                    for m in range(KT):
                        last = mm(pb[2][:, m * SLOTS:(m + 1) * SLOTS], dn_ring[4 * j + c][:, kk, m * P:(m + 1) * P],
                                  hT[:, 2 * c + kk], c == 0 and kk == 0 and m == 0, c == 3 and kk == 1,
                                  skip_group_check=True)
                last.then_inc(S("dn_used"), 1)

        def combine(b, y_wait, xe_wait):
            pe.wait_ge(S("y_done"), y_wait)
            for k in range(KT):
                last = pe.transpose(pb[5 + k // 4][:, (k % 4) * P:(k % 4 + 1) * P], ye_T[:, k], ident[:])
                if k % 4 == 3:
                    last.then_inc(S("y_turned"), 1)
            pe.wait_ge(S("goh_ready"), b + 1)
            for t, (f, n) in enumerate(TT):
                last = pe.transpose(pb[7][:, f:f + n], goh[0:n, t], ident[0:n, 0:n])
            last.then_inc(S("g_turned"), 1)
            pe.wait_ge(S("gT_ready"), b + 1)
            pe.wait_ge(S("xe_ready"), xe_wait)
            for m in range(KT):
                if m % 4 == 0:
                    pe.wait_ge(S("ye_ready"), b * 2 + (1 + m // 4))
                if m >= 2:
                    pe.wait_ge(S("acc_done"), b * 8 + (m - 1))
                mm(pb[3 + m % 2][:, 0:T], ye[:, m * P:(m + 1) * P], gT[:], True, True).then_inc(S("comb_done"), 1)

        def pe_round(r):
            if not isinstance(r, int):
                pe.wait_ge(S("acc_done"), r * (8 * 17))
            gather(r * 17)
            with pe.Fori(0, PAIRS) as i:
                n = dict(n=i + r * PAIRS, g=i + r * 17, e2=i * 2 + (r * NE + 1))
                gate_up(n, 0)
                combine(i + r * 17, i * 2 + (r * NE + 1), (i + r * 17) * 2 + 2)
                down(n, 0)
                gate_up(n, 1)
                pe.wait_ge(S("acc_done"), (i + r * 17) * 8 + 8)
                gather(i + (r * 17 + 1))
                down(n, 1)
            combine(r * 17 + PAIRS, r * NE + (NE + 1), (r * 17 + PAIRS) * 2 + 2)

        pe_round(0)
        pe.wait_ge(S("route_ready"), 1)
        n = pe.alloc_register("pe_max_count")
        pe.reg_load(n, flag[0:1, 0:1])
        with pe.If_cmp(n, SLOTS, "IS_GT"):
            with pe.Fori(1, ROUNDS) as r:
                pe_round(r)

    @block.scalar
    def _(act):
        A = nc.scalar.activation
        for dst, src, s in ((cols, "cols", "cols_in"), (par, "par", "par_in"), (b_raw, "b_raw", "b_in")):
            act.dma_start(dst[:], a[src]).then_inc(S(s), 16)
        for dst, src in ((ident, "ident"), (ones, "ones"), (block_ones, "block_ones"), (tri, "tri"),
                         (scan_pat, "scan_pat"), (iota, "iota")):
            act.dma_start(dst[:], a[src]).then_inc(S("const_in"), 16)
        act.dma_start(h0[:], a["h0"]).then_inc(S("h0_in"), 16)
        act.dma_start(cT[:, 0], a["c_re"]).then_inc(S("c_in"), 16)
        act.dma_start(cT[:, 2], a["c_im"]).then_inc(S("c_in"), 16)
        for k in range(KT):
            act.wait_ge(x_in[k // 4], 16)
            A(xsq[:, k], xT[:, k], ACT.Square).then_inc(S("xsq_ready"), 1)
        act.wait_ge(S("par_in"), 16)
        A(par_t[0][:], par[:, 2], ACT.Exp).then_inc(S("par_act"), 1)
        act.wait_ge(S("par_dve"), 1)
        A(par_t[2][:], par_t[1][:], ACT.Exp).then_inc(S("par_act"), 1)
        act.wait_ge(S("par_dve"), 2)
        A(par_t[5][:], par_t[3][:], ACT.Sin).then_inc(S("par_act"), 1)
        A(par_t[6][:], par_t[4][:], ACT.Sin).then_inc(S("par_act"), 1)

        def rsqrt(dst, src, tmp, waits, signal):
            for s, v in waits:
                act.wait_ge(S(s), v)
            ordered(act, "act", A(tmp, src, ACT.Ln))
            A(dst, tmp, ACT.Exp, scale=-0.5).then_inc(S(signal), 1)

        rsqrt(r_mix[:], ms[:], r_mix[:], [("ms_ready", 1)], "r_mix_ready")
        for i in range(5):
            act.wait_ge(S("proj_done"), i + 1)
            bank = pb[5 + i % 2][:, 0:T]
            if i:
                act.wait_ge(S("qk_sum"), i)
            A(qsq[:], bank, ACT.Square).then_inc(S("sq_ready"), 1)
            A(qT[:, i] if i < 4 else kT[:], bank, ACT.Copy, scale=col(C_GQ if i < 4 else C_GK)).then_inc(
                S("proj_free"), 1)
            if i:
                rsqrt(vv[:], vv[:], vv[:], [("vv_ready", i)], "rq_ready")
        rsqrt(vv[:], vv[:], vv[:], [("vv_ready", 5)], "rq_ready")
        act.wait_ge(S("qk_ready"), 4)
        A(q_s[:].rearrange("p (i q) -> p i q", i=CT), qT[:, :, NP:T], ACT.Copy).then_inc(S("qs_ready"), 1)
        act.wait_ge(S("tab_dve"), 1)
        for x in range(2):
            A(cs[:, :, x, NP:T].rearrange("p t (b s) -> p t b s", b=NB), wide(e_tab[:, x, :, 0:NS], 2, NB),
              ACT.Copy).then_inc(S("tab_act"), 1)

        def scan_factor(t):
            if t >= 2:
                act.wait_ge(S("g_ready"), t - 1)
            A(r_scan[t % 2][:], wide(scan_pat[:], 1, 2), ACT.Copy, scale=mag[:, t:t + 1]).then_inc(
                S("r_scan_ready"), 1)

        def softmax_part(n):
            if n == 0:
                pieces = [(s_p0[:, i], i) for i in range(8)]
            elif n == 1:
                pieces = [(s_p1[:, i], 8 + i) for i in range(8)]
            else:
                pieces = [(s_s[:, n - 2], 14 + n)]
            act.wait_ge(S("neg_ready"), 1)
            for k, (ap, i) in enumerate(pieces):
                last = A(ap, ap, ACT.Exp, bias=st_neg[:, i:i + 1], accum_out=st_sum[:, i:i + 1])
            last.then_inc(S("exp_done"), 1)

        def weights(n):
            if n == 0:
                pieces = [(s_p0[:, i], i) for i in range(8)]
            elif n == 1:
                pieces = [(s_p1[:, i], 8 + i) for i in range(8)]
            else:
                pieces = [(s_s[:, n - 2], 14 + n)]
            act.wait_ge(S("sum_inv"), 1)
            for ap, i in pieces:
                last = A(ap, ap, ACT.Copy, scale=st_sum[:, i:i + 1])
            last.then_inc(S("p_ready"), 1)

        act.wait_ge(S("const_in"), 96)
        act.wait_ge(S("tab_dve"), 2)
        for t in range(SLOTS_N):
            if t < ST:
                scan_factor(t)
            if t == 4:
                act.wait_ge(S("neg_ready"), 1)
                for k in range(4):
                    softmax_part(k)
                A(st_snk[:], st_snk[:], ACT.Exp).then_inc(S("exp_done"), 1)
            if t == 5:
                for k in range(4):
                    weights(k)
            for n in TURN_SLOT.get(t, ()):
                act.wait_ge(S("pt_turned"), n + 1)
                kind = TURNS[n][0]
                rows, width = (NSAMP, P) if kind == "n" else (P, 512)
                A(pT[0:rows, PT_AT[n] * P:PT_AT[n] * P + width], pb[5 + n % 2][0:rows, 0:width], ACT.Copy).then_inc(
                    S("pt_ready"), 1)
            if t == PV_SLOT:
                for n in range(3):
                    act.wait_ge(S("pv_ready"), n + 1)
                    w = P if n < 2 else NSAMP
                    A(aT[:, :, n * P:n * P + w], pb[5 + n % 2][:, 0:4 * w].rearrange("p (i q) -> p i q", i=4),
                      ACT.Copy).then_inc(S("a_part_ready"), 1)
            if t == ASUM_SLOT:
                act.wait_ge(S("a_part_ready"), 3)
                for c in range(CT):
                    A(pT_sq(c), aT[:, c], ACT.Square).then_inc(S("asq_ready"), 1)
                rsqrt(pT[:, 1536:1536 + T], pT[:, 1536:1536 + T], pT[:, 1536:1536 + T], [("av_ready", 1)], "ar_ready")
            if t >= 2 and (t - 2) % 4 == 3:
                gelu_square(act, (t - 2) // 4)
                gelu_tanh(act, (t - 2) // 4)
        act.wait_ge(S("rot_ready"), 2 * ST)
        for c in range(CT):
            act.wait_ge(S("glu_done"), 2 * c + 1)
            if c >= 2:
                act.wait_ge(S("s_ready"), c - 1)
            A(v_glu(0, c), pb[(2 * c) % 4][:, 0:T], ACT.Identity, scale=0.5, bias=col(C_BA + c)).then_inc(S("ga_ready"), 1)
            act.wait_ge(S("glu_done"), 2 * c + 2)
            A(v_glu(1, c), pb[(2 * c + 1) % 4][:, 0:T], ACT.Tanh, scale=0.25, bias=col(C_BG + c)).then_inc(S("th_glu"), 1)
            if c:
                act.wait_ge(S("s_ready"), c)
                A(vsq(c - 1), uT[:, c - 1], ACT.Square).then_inc(S("ssq_ready"), 1)
        act.wait_ge(S("s_ready"), CT)
        A(vsq(CT - 1), uT[:, CT - 1], ACT.Square).then_inc(S("ssq_ready"), 1)
        rsqrt(v_rot[:, 0], v_rot[:, 0], v_rot[:, 0], [("sv_ready", 1)], "sr_ready")
        for k in range(KT):
            act.wait_ge(S("x2_ready"), k + 1)
            if k >= 2:
                act.wait_ge(S("x2sum_ready"), k - 1)
            if k == 0:
                act.wait_ge(S("sn_ready"), CT)
            A(x2sq[:, k % 2], xT[:, k], ACT.Square).then_inc(S("x2sq_ready"), 1)
        rsqrt(r2[:], r2[:], r2[:], [("x2v_ready", 1)], "r2_ready")
        for u in range(6):
            act.wait_ge(S("xtok_turned"), u + 1)
            if u == 0:
                act.wait_ge(S("outB_done"), KT)
            n = TT[u // 2][1]
            A(x_tok[u // 2][0:n, (u % 2) * 512:(u % 2 + 1) * 512], pb[(0, 1, 2, 3, 6, 7)[u]][0:n, :], ACT.Copy).then_inc(
                S("xtok_ready"), 1)
            if u == 3:
                act.wait_ge(S("top_ready"), 1)
                A(ex4[:], ex4[:], ACT.Exp).then_inc(S("exp4_done"), 1)

        def to_experts(g):
            for h in range(2):
                act.wait_ge(S("gathered"), g * 2 + (h + 1))
                A(xe[:, 4 * h:4 * h + 4].rearrange("p k s -> p (k s)"), pb[3 + h][:], ACT.Copy).then_inc(S("xe_ready"), 1)

        def act_combine(b):
            for h in range(2):
                act.wait_ge(S("y_turned"), b * 2 + (h + 1))
                A(ye[:, 512 * h:512 * h + 512], pb[5 + h][:], ACT.Copy).then_inc(S("ye_ready"), 1)
            act.wait_ge(S("g_turned"), b + 2)
            A(gT[:], pb[7][:, 0:T], ACT.Copy).then_inc(S("gT_ready"), 1)

        def act_tanh(e):
            act.wait_ge(S("hg_ready"), e + 1)
            A(th[:], hg[:], ACT.Tanh, scale=0.851).then_inc(S("th_ready"), 1)

        def act_round(r):
            to_experts(r * 17)
            with act.Fori(0, PAIRS) as i:
                act_combine(i + r * 17)
                act_tanh(i * 2 + r * NE)
                act_tanh(i * 2 + (r * NE + 1))
                to_experts(i + (r * 17 + 1))
            act_combine(r * 17 + PAIRS)

        act_round(0)
        act.wait_ge(S("route_ready"), 1)
        n = act.alloc_register("act_max_count")
        act.reg_load(n, flag[0:1, 0:1])
        with act.If_cmp(n, SLOTS, "IS_GT"):
            with act.Fori(1, ROUNDS) as r:
                act_round(r)

    @block.vector
    def _(dve):
        V = nc.vector

        def link(ins):
            ordered(dve, "dve", ins)

        dve.wait_ge(S("cols_in"), 16)
        link(V.tensor_scalar(cols[:, C_BG:C_BG + CT], cols[:, C_BG:C_BG + CT], 0.5, None, ALU.mult))
        for k in range(KT):
            dve.wait_ge(x_in[k // 4], 16)
            V.tensor_scalar(xg[:, k], xT[:, k], col(C_GMIX + k), None, ALU.mult).then_inc(S("xg_ready"), 1)
        dt, lrd, amag, ang, coang, sn, cn, ta, tb, tc, td = [x[:] for x in par_t]
        l_re, l_im = par[:, 0], par[:, 1]
        dve.wait_ge(S("par_in"), 16)
        link(V.tensor_scalar(l_re, l_re, -1e-4, None, ALU.min))
        dve.wait_ge(S("par_act"), 1)
        V.tensor_tensor(lrd, l_re, dt, ALU.mult).then_inc(S("par_dve"), 1)
        link(V.tensor_tensor(ta, l_im, dt, ALU.mult))
        link(V.tensor_scalar(tb, ta, 1 / TWO_PI, ROUND_MAGIC, ALU.mult, ALU.add))
        link(V.tensor_scalar(tb, tb, ROUND_MAGIC, None, ALU.subtract))
        link(V.scalar_tensor_tensor(out=ta, in0=tb, scalar=-TWO_PI_HI, in1=ta, op0=ALU.mult, op1=ALU.add))
        link(V.scalar_tensor_tensor(out=ta, in0=tb, scalar=-TWO_PI_LO, in1=ta, op0=ALU.mult, op1=ALU.add))
        link(V.tensor_scalar(ang, ta, 3.1415925, -3.1415925, ALU.min, ALU.max))
        link(V.tensor_scalar(tb, ang, -1.0, None, ALU.mult))
        link(V.tensor_tensor(tb, tb, ang, ALU.max))
        V.tensor_scalar(coang, tb, -1.0, float(np.pi / 2), ALU.mult, ALU.add).then_inc(S("par_dve"), 1)
        dve.wait_ge(S("sum_ready"), 1)
        V.tensor_scalar(ms[:], pb[4][:, 0:T], 1 / D, EPS, ALU.mult, ALU.add).then_inc(S("ms_ready"), 1)
        dve.wait_ge(S("par_act"), 4)
        V.tensor_copy(mag[:], amag[:, 0:ST])
        V.tensor_copy(e_tab[:, 0, :, 0], cn[:, 0:ST])
        link(V.tensor_copy(e_tab[:, 1, :, 0], sn[:, 0:ST]))

        dve.wait_ge(S("den_ready"), 1)
        V.reciprocal(coang[:, ST:], ang[:, ST:]).then_inc(S("den_inv"), 1)

        def powers(tab, first, m, n, end=False):
            src = tab[:, :, :, first:first + n]
            k = first + m - 1
            o1, o2 = t1[:, :, :, 0:n], t2[:, :, :, 0:n]
            re = wide(wide(tab[:, 0, :, k], 1, 2), 3, n)
            im = wide(wide(tab[:, 1, :, k], 1, 2), 3, n)
            V.tensor_tensor(o1, src, re, ALU.mult)
            link(V.tensor_tensor(o2, src, im, ALU.mult))
            d = slice(first + m, first + m + n)
            V.tensor_tensor(tab[:, 0, :, d], o1[:, 0], o2[:, 1], ALU.subtract)
            last = V.tensor_tensor(tab[:, 1, :, d], o1[:, 1], o2[:, 0], ALU.add)
            if not end:
                link(last)
            return last

        for m in (1, 2, 4, 8):
            powers(e_tab, 0, m, m)
        V.memset(f_tab[:, 0, :, 0], 1.0)
        V.memset(f_tab[:, 1, :, 0], 0.0)
        link(V.tensor_copy(f_tab[:, :, :, 1], e_tab[:, :, :, 15]))
        for m in (1, 2, 4, 8):
            last = powers(f_tab, 1, m, min(m, 15 - m), m == 8)
        last.then_inc(S("tab_dve"), 1)
        dve.wait_ge(S("tab_dve"), 1)
        dve.wait_ge(S("r_mix_ready"), 1)
        for c in range(CT):
            dve.wait_ge(S("u_proj"), c + 1)
            V.tensor_tensor(uT[:, c], pb[c][:, 0:T], r_mix[:], ALU.mult).then_inc(S("u_ready"), 1)
        qk = [0]

        def qk_step():
            i = qk[0]
            qk[0] += 1
            dve.wait_ge(S("qk_sum"), i + 1)
            if i == 0:
                V.tensor_scalar(ms[:], ms[:], EPS * HD, None, ALU.mult).then_inc(S("ms_ready"), 1)
            dve.wait_ge(S("ms_ready"), 2)
            if i:
                dve.wait_ge(S("qk_ready"), i)
            link(V.tensor_tensor(vv[:], pb[7][:, 0:T], ms[:], ALU.add))
            V.tensor_scalar(vv[:], vv[:], 1 / HD, None, ALU.mult).then_inc(S("vv_ready"), 1)
            dve.wait_ge(S("rq_ready"), i + 1)
            dst = qT[:, i] if i < 4 else kT[:]
            V.tensor_tensor(dst, dst, vv[:], ALU.mult).then_inc(S("qk_ready"), 1)

        for t in range(ST // 2):
            last = table(V, dve, t, tab_tmp, "dve")
            if t == ST // 2 - 1:
                last.then_inc(S("tab_dve"), 1)
                dve.wait_ge(S("tab_dve"), 2)
            else:
                link(last)
            if t in (1, 3, 5):
                qk_step()
        qk_step()
        qk_step()
        dve.wait_ge(S("proj_done"), 6)
        V.tensor_tensor(vT[:], pb[6][:, 0:T], r_mix[:], ALU.mult).then_inc(S("v_ready"), 1)
        dve.wait_ge(S("v_turned"), 3)
        for t, (f, n) in enumerate(TT):
            V.tensor_copy(v_tok[0:n, t], pb[7][0:n, t * P:(t + 1) * P]).then_inc(S("v_tok_ready"), 1)

        def ssm_tile(t):
            b = 2 * (t % 2)
            w_re, w_im = pb[b][:, 0:T], pb[b + 1][:, 0:T]
            cos, sin = cs[:, t, 0], cs[:, t, 1]
            if t == 0:
                dve.wait_ge(S("tab_act"), 2)
            if t == ST // 2:
                dve.wait_ge(S("tab_pool"), 1)
            if t == 0:
                dve.wait_ge(S("h0_scaled"), 1)
                dve.wait_ge(S("bbar_ready"), 1)
            dve.wait_ge(S("w_ready"), t + 1)
            V.tensor_tensor(p1[:, 0], w_re, cos, ALU.mult)
            V.tensor_tensor(p1[:, 1], w_im, cos, ALU.mult)
            V.tensor_tensor(p2[:, 0], w_re, sin, ALU.mult)
            V.tensor_tensor(p2[:, 1], w_im, sin, ALU.mult).then_inc(S("w_free"), 1)
            dve.wait_ge(S("w_free"), t + 1)
            V.tensor_tensor(v_rot[:, 0], p1[:, 0], p2[:, 1], ALU.add)
            link(V.tensor_tensor(v_rot[:, 1], p1[:, 1], p2[:, 0], ALU.subtract))
            first = v_rot[:, :, NP:T:NS]
            link(V.tensor_tensor(first, first, h0[:, t], ALU.add))
            dve.wait_ge(S("r_scan_ready"), t + 1)
            if t >= 2:
                dve.wait_ge(S("rot_ready"), 2 * (t - 1))
            V.tensor_tensor_scan(g_rot[t % 2][:].rearrange("p x t -> p (x t)"),
                                 r_scan[t % 2][:].rearrange("p x t -> p (x t)"),
                                 v_rot[:].rearrange("p x t -> p (x t)"), 0.0, ALU.mult, ALU.add).then_inc(S("g_ready"), 1)

        def masked_scores(n):
            kind, kv, part = SCORES[n]
            bank = pb[5 + n % 2]
            dve.wait_ge(S("score_ready"), n + 1)
            if n == 0:
                dve.wait_ge(S("mask_in"), 32)
            sc = HD ** -0.5
            if kind == "p0":
                ops = [(s_p0[:, 4 * kv + i], bank[:, i * P:(i + 1) * P], mask_p[:, P:2 * P], 4 * kv + i) for i in range(4)]
            elif kind == "p1":
                ops = [(s_p1[:, 4 * kv + 2 * part + i], bank[:, i * 2 * P:(i + 1) * 2 * P], mask_p[:],
                        8 + 4 * kv + 2 * part + i) for i in range(2)]
            elif kind == "s":
                f = part * 512
                ops = [(s_s[:, kv, f:f + 512], bank[:], mask_s[:, f:f + 512], 16 + 3 * kv + part)]
            else:
                ops = [(s_s[:, kv, NB * WIN:], bank[:, 0:NSAMP], mask_s[:, NB * WIN:], 18 + 3 * kv)]
            for out, ps, mask, k in ops:
                last = V.tensor_tensor_reduce(out, ps, mask, sc, -3e38, ALU.add, ALU.max, st_mx[:, k:k + 1])
            last.then_inc(S("score_used"), 1)

        def maxima():
            dve.wait_ge(S("score_used"), 12)
            link(V.tensor_reduce(st_mx[:, 22:24], st_mx[:, 16:22].rearrange("p (k j) -> p k j", k=2), AX.X, ALU.max))
            sink8 = cols[:, C_SINK:C_SINK + 8]
            V.tensor_tensor(st_neg[:, 0:8], st_mx[:, 0:8], sink8, ALU.max)
            V.tensor_tensor(st_neg[:, 8:16], st_mx[:, 8:16], sink8, ALU.max)
            link(V.tensor_tensor(st_neg[:, 16:18], st_mx[:, 22:24], cols[:, C_SINK + 8:C_SINK + 10], ALU.max))
            V.tensor_tensor(st_snk[:, 0:8], sink8, st_neg[:, 0:8], ALU.subtract)
            V.tensor_tensor(st_snk[:, 8:16], sink8, st_neg[:, 8:16], ALU.subtract)
            link(V.tensor_tensor(st_snk[:, 16:18], cols[:, C_SINK + 8:C_SINK + 10], st_neg[:, 16:18], ALU.subtract))
            V.tensor_scalar(st_neg[:], st_neg[:], -1.0, None, ALU.mult).then_inc(S("neg_ready"), 1)

        def norm_finish(bank, dst, n, eps, ready, signal):
            dve.wait_ge(S(ready), 1)
            V.tensor_scalar(dst, pb[bank][:, 0:T], 1 / n, eps, ALU.mult, ALU.add).then_inc(S(signal), 1)

        def y_part(c):
            dve.wait_ge(S("rot_used"), 4 * c + 4)
            V.scalar_tensor_tensor(out=yT[:, c], in0=uT[:, c], scalar=col(C_D + c), in1=pb[4 + 3 * (c % 2)][:, 0:T],
                                   op0=ALU.mult, op1=ALU.add).then_inc(S("y_ready"), 1)

        def gelu_poly(c):
            dve.wait_ge(S("ysq_ready"), c + 1)
            link(V.tensor_scalar(gelu_tmp(c), gelu_tmp(c), 0.044715, 1.0, ALU.mult, ALU.add))
            V.tensor_tensor(gelu_tmp(c), gelu_tmp(c), yT[:, c], ALU.mult).then_inc(S("y_poly"), 1)

        def gelu_end(c):
            dve.wait_ge(S("tanh_ready"), c + 1)
            V.scalar_tensor_tensor(out=yT[:, c], in0=gelu_tmp(c), scalar=1.0, in1=yT[:, c], op0=ALU.add,
                                   op1=ALU.mult).then_inc(S("gelu_ready"), 1)

        for t in range(SLOTS_N):
            if t < ST:
                ssm_tile(t)
            for n in SCORE_SLOT.get(t, ()):
                masked_scores(n)
            if t == 3:
                maxima()
            if t == 5:
                dve.wait_ge(S("exp_done"), 5)
                link(V.tensor_tensor(st_sum[:], st_sum[:], st_snk[:], ALU.add))
                V.reciprocal(st_sum[:], st_sum[:]).then_inc(S("sum_inv"), 1)
            if t == ASUM_SLOT:
                norm_finish(6, pT[:, 1536:1536 + T], DS, EPS, "asum_ready", "av_ready")
            if t == ASUM_SLOT + 1:
                dve.wait_ge(S("ar_ready"), 1)
                for c in range(CT):
                    V.scalar_tensor_tensor(out=aT[:, c], in0=aT[:, c], scalar=col(C_GATT + c), in1=pT[:, 1536:1536 + T],
                                           op0=ALU.mult, op1=ALU.mult).then_inc(S("an_ready"), 1)
            for m in OUTA_SLOT.get(t, ()):
                dve.wait_ge(S("outA_done"), m + 1)
                V.tensor_tensor(xT[:, m], xT[:, m], pb[5 + m % 2][:, 0:T], ALU.add).then_inc(S("xmid_ready"), 1)
            if t >= 2 and (t - 2) % 4 == 3:
                c = (t - 2) // 4
                y_part(c)
                gelu_poly(c)
                gelu_end(c)
        for c in range(CT):
            dve.wait_ge(S("ga_ready"), c + 1)
            dve.wait_ge(S("th_glu"), c + 1)
            V.scalar_tensor_tensor(out=uT[:, c], in0=v_glu(1, c), scalar=1.0, in1=v_glu(0, c), op0=ALU.add,
                                   op1=ALU.mult).then_inc(S("s_ready"), 1)
        norm_finish(4, v_rot[:, 0], DS, 4 * EPS, "ssum_ready", "sv_ready")
        dve.wait_ge(S("sr_ready"), 1)
        for c in range(CT):
            V.scalar_tensor_tensor(out=uT[:, c], in0=uT[:, c], scalar=col(C_GSSM + c), in1=v_rot[:, 0],
                                   op0=ALU.mult, op1=ALU.mult).then_inc(S("sn_ready"), 1)
        dve.wait_ge(S("xmid_ready"), KT)
        for m in range(KT):
            dve.wait_ge(S("outB_done"), m + 1)
            V.tensor_tensor(xT[:, m], xT[:, m], pb[m % 4][:, 0:T], ALU.add).then_inc(S("x2_ready"), 1)
        dve.wait_ge(S("x2sum_ready"), KT)
        V.tensor_scalar(r2[:], pb[4][:, 0:T], 1 / D, EPS, ALU.mult, ALU.add).then_inc(S("x2v_ready"), 1)
        V.memset(lg[:], 0.0)
        V.memset(pos[:], -1.0).then_inc(S("gu_free"), 1)
        V.memset(gate[:], 0.0).then_inc(S("g_turned"), 1)
        V.memset(ye_T[:], 0.0).then_inc(S("y_done"), 1)
        dve.wait_ge(S("x2_ready"), KT)
        dve.wait_ge(S("r2_ready"), 1)
        for k in range(KT):
            V.scalar_tensor_tensor(out=xg[:, k], in0=xT[:, k], scalar=col(C_GFFN + k), in1=r2[:],
                                   op0=ALU.mult, op1=ALU.mult).then_inc(S("xn_ready"), 1)
        dve.wait_ge(S("logits_ready"), 3)
        dve.wait_ge(S("y_done"), 1)
        bias = cols[:, C_BR:C_BR + NE]
        V.tensor_tensor(lg[:, 0:2], pb[5][:, 0:2 * NE].rearrange("p (t e) -> p t e", t=2), wide(bias, 1, 2), ALU.add)
        link(V.tensor_tensor(lg[0:NSAMP, 2], pb[5][0:NSAMP, 2 * NE:3 * NE], bias[0:NSAMP], ALU.add))
        for t in range(3):
            last = V.max(v8[:, t], lg[:, t])
        link(last)
        for t in range(3):
            last = V.max_index(i8[:, t], v8[:, t], lg[:, t])
        link(last)
        V.tensor_copy(if8[:], i8[:])
        V.tensor_tensor(ex4[:], v8[:, :, 0:4], wide(v8[:, :, 0], 2, 4), ALU.subtract).then_inc(S("top_ready"), 1)
        iota_e = wide(iota[:, 0:NE], 1, 3)
        dve.wait_ge(S("top_ready"), 1)
        for k in range(TOPK):
            if k == 0:
                link(V.tensor_tensor(sel[:], iota_e, wide(if8[:, :, 0], 2, NE), ALU.is_equal))
            else:
                link(V.tensor_tensor(eq[:], iota_e, wide(if8[:, :, k], 2, NE), ALU.is_equal))
                link(V.tensor_tensor(sel[:], sel[:], eq[:], ALU.add))
        V.tensor_scalar(sel[:, 2], sel[:, 2], tri[:, NSAMP:NSAMP + 1], None, ALU.mult).then_inc(S("sel_ready"), 1)
        dve.wait_ge(S("exp4_done"), 1)
        link(V.tensor_reduce(gs[:], ex4[:], AX.X, ALU.add))
        link(V.reciprocal(gs[:], gs[:]))
        link(V.tensor_tensor(ex4[:], ex4[:], wide(gs[:], 2, 4), ALU.mult))
        G = gate[:, :, 2:2 + NE]
        for k in range(TOPK):
            link(V.tensor_tensor(eq[:], iota_e, wide(if8[:, :, k], 2, NE), ALU.is_equal))
            link(V.tensor_tensor(eq[:], eq[:], wide(ex4[:, :, k], 2, NE), ALU.mult))
            link(V.tensor_tensor(G, G, eq[:], ALU.add))
        dve.wait_ge(S("pos_ready"), 1)
        dve.wait_ge(S("sel_ready"), 1)
        Q = pos[:, :, 2:2 + NE]
        link(V.scalar_tensor_tensor(out=Q, in0=pb[4][:, 0:3 * NE].rearrange("p (t e) -> p t e", t=3), scalar=1.0,
                                    in1=sel[:], op0=ALU.add, op1=ALU.mult))
        V.tensor_scalar(Q, Q, 1.0, None, ALU.subtract)
        link(V.tensor_reduce(cnt[:, 0:1], pb[4][:, 3 * NE:4 * NE], AX.X, ALU.max))
        V.tensor_copy(flag[:, 0:1], cnt[:, 0:1]).then_inc(S("route_ready"), 1)
        dve.wait_ge(S("route_ready"), 1)

        def one_hot(dst, c):
            return V.tensor_tensor(dst[:].rearrange("p t (j s) -> p t j s", j=2),
                                   wide(wide(iota[:], 1, 2), 1, 3), wide(pos[:, :, bass.ds(c, 2)], 3, SLOTS),
                                   ALU.is_equal)

        def build_oh(c, g, first=False):
            if not first:
                dve.wait_ge(S("gathered"), g * 2)
            one_hot(oh, c).then_inc(S("oh_ready"), 1)

        def hidden(e, j, i, r):
            ei = i * 2 + j
            dve.wait_ge(S("gu_used"), e * 8 + 8)
            V.tensor_tensor(hg[:], pb[0][:].rearrange("p (m s) -> p m s", m=8), wide(b_gu[:, bass.ds(ei * 16, 8)], 2, SLOTS), ALU.add)
            V.tensor_tensor(hl[:], pb[1][:].rearrange("p (m s) -> p m s", m=8), wide(b_gu[:, bass.ds(ei * 16 + 8, 8)], 2, SLOTS),
                            ALU.add).then_inc(S("gu_free"), 1)
            dve.wait_ge(S("gu_free"), e + 2)
            V.tensor_scalar(hg[:], hg[:], 7.0, None, ALU.min).then_inc(S("hg_ready"), 1)
            V.tensor_scalar(hl[:], hl[:], 7.0, -7.0, ALU.min, ALU.max).then_inc(S("hl_ready"), 1)
            dve.wait_ge(S("hl_ready"), e + 1)
            V.scalar_tensor_tensor(out=hl[:], in0=hl[:], scalar=1.0, in1=hg[:], op0=ALU.add, op1=ALU.mult).then_inc(
                S("hlg_ready"), 1)
            dve.wait_ge(S("hlg_ready"), e + 1)
            dve.wait_ge(S("th_ready"), e + 1)
            V.scalar_tensor_tensor(out=hT[:], in0=th[:], scalar=1.0, in1=hl[:], op0=ALU.add, op1=ALU.mult).then_inc(
                S("h_ready"), 1)

        def expert_out(e, j, i):
            dve.wait_ge(S("dn_used"), e * 4 + 4)
            bd = b_dn[:, bass.ds((i * 2 + j) * 8, 8)]
            V.scalar_tensor_tensor(out=ye_T[:, :, j], in0=pb[2][:].rearrange("p (m s) -> p m s", m=8), scalar=0.5,
                                   in1=wide(bd, 2, SLOTS), op0=ALU.mult, op1=ALU.add).then_inc(S("y_done"), 1)

        def accumulate(b):
            for m in range(KT):
                dve.wait_ge(S("comb_done"), b * 8 + (m + 1))
                V.tensor_tensor(xT[:, m], xT[:, m], pb[3 + m % 2][:, 0:T], ALU.add).then_inc(S("acc_done"), 1)

        def gated(c, b):
            dve.wait_ge(S("g_turned"), b + 1)
            one_hot(goh, c).then_inc(S("goh_step"), 1)
            dve.wait_ge(S("goh_step"), b + 1)
            v = goh[:].rearrange("p t (j s) -> p t j s", j=2)
            V.tensor_tensor(v, v, wide(gate[:, :, bass.ds(c, 2)], 3, SLOTS), ALU.mult).then_inc(S("goh_ready"), 1)

        def dve_round(r):
            if not isinstance(r, int):
                dve.wait_ge(S("acc_done"), r * (8 * 17))
                V.tensor_scalar(pos[:], pos[:], float(SLOTS), None, ALU.subtract).then_inc(S("pos_moved"), 1)
                dve.wait_ge(S("pos_moved"), r)
                build_oh(2, r * 17)
            else:
                build_oh(2, 0, True)
            with dve.Fori(0, PAIRS) as i:
                gated(i * 2, i + r * 17)
                hidden(i * 2 + r * NE, 0, i, r)
                accumulate(i + r * 17)
                expert_out(i * 2 + r * NE, 0, i)
                build_oh(i * 2 + 4, i + (r * 17 + 1))
                hidden(i * 2 + (r * NE + 1), 1, i, r)
                expert_out(i * 2 + (r * NE + 1), 1, i)
            gated(2 * PAIRS, r * 17 + PAIRS)
            accumulate(r * 17 + PAIRS)

        dve.wait_ge(S("moe_in"), 32)
        dve_round(0)
        n = dve.alloc_register("dve_max_count")
        dve.reg_load(n, flag[0:1, 0:1])
        with dve.If_cmp(n, SLOTS, "IS_GT"):
            with dve.Fori(1, ROUNDS) as r:
                dve_round(r)
        V.tensor_copy(cnt[:, 1:2], cnt[:, 0:1]).then_inc(S("result_ready"), 1)

    @block.gpsimd
    def _(pool):
        G = nc.gpsimd

        def link(ins):
            ordered(pool, "pool", ins)

        pool.wait_ge(S("c_in"), 32)
        G.tensor_scalar(cT[:, 1], cT[:, 0], -1.0, None, ALU.mult).then_inc(S("c_neg"), 1)
        G.tensor_scalar(cT[:, 2], cT[:, 2], -1.0, None, ALU.mult).then_inc(S("c_neg"), 1)
        lo = ST
        dt, lrd, amag, ang, coang, sn, cn, ta, tb, tc, td = [x[:, lo:] for x in par_t]
        l_re, l_im = par[:, 0, lo:], par[:, 1, lo:]
        pool.wait_ge(S("par_act"), 4)
        pool.wait_ge(S("par_dve"), 2)
        G.tensor_tensor(lrd, amag, cn, ALU.mult)
        G.tensor_tensor(ang, l_re, l_re, ALU.mult)
        link(G.tensor_tensor(tc, amag, sn, ALU.mult))
        G.tensor_tensor(coang, l_im, l_im, ALU.mult)
        link(G.tensor_scalar(lrd, lrd, 1.0, None, ALU.subtract))
        G.tensor_tensor(ang, ang, coang, ALU.add).then_inc(S("den_ready"), 1)
        G.tensor_tensor(ta, lrd, l_re, ALU.mult)
        link(G.tensor_tensor(tb, tc, l_im, ALU.mult))
        link(G.tensor_tensor(ta, ta, tb, ALU.add))
        G.tensor_tensor(tb, tc, l_re, ALU.mult)
        link(G.tensor_tensor(td, lrd, l_im, ALU.mult))
        link(G.tensor_tensor(tb, tb, td, ALU.subtract))
        pool.wait_ge(S("den_inv"), 1)
        G.tensor_tensor(ta, ta, coang, ALU.mult)
        link(G.tensor_tensor(tb, tb, coang, ALU.mult))
        pool.wait_ge(S("b_in"), 16)

        def z(ap):
            return wide(ap.rearrange("p (c s) -> p c s", c=CT), 2, 2)

        def m4(ap):
            return ap.rearrange("p c (h s) -> p c h s", h=2)

        G.tensor_tensor(m4(b_bar[:, 0]), m4(b_raw[:, 0]), z(ta), ALU.mult)
        G.tensor_tensor(m4(bb_tmp[:, 0]), m4(b_raw[:, 1]), z(tb), ALU.mult)
        G.tensor_tensor(m4(b_bar[:, 1]), m4(b_raw[:, 1]), z(ta), ALU.mult)
        link(G.tensor_tensor(m4(bb_tmp[:, 1]), m4(b_raw[:, 0]), z(tb), ALU.mult))
        link(G.tensor_tensor(b_bar[:, 0], b_bar[:, 0], bb_tmp[:, 0], ALU.subtract))
        G.tensor_tensor(b_bar[:, 1], b_bar[:, 1], bb_tmp[:, 1], ALU.add).then_inc(S("bbar_ready"), 1)
        pool.wait_ge(S("bbar_ready"), 1)
        pool.wait_ge(S("h0_in"), 16)
        pool.wait_ge(S("tab_dve"), 1)
        G.tensor_tensor(h0[:], h0[:], wide(wide(mag[:], 2, NB), 2, 2), ALU.mult).then_inc(S("h0_scaled"), 1)
        pool.wait_ge(S("h0_scaled"), 1)
        for t in range(ST // 2, ST):
            last = table(G, pool, t, tab_tmp_p, "pool")
            if t == ST - 1:
                last.then_inc(S("tab_pool"), 1)
                pool.wait_ge(S("tab_pool"), 1)
            else:
                link(last)

        for t in range(ST):
            if t >= 2:
                pool.wait_ge(S("rot_used"), t - 1)
            pool.wait_ge(S("g_ready"), t + 1)
            q = q_rot[t % 2]
            g = g_rot[t % 2]
            for x in range(2):
                G.tensor_tensor(q[:, x], g[:], wide(cs[:, t, x], 1, 2), ALU.mult).then_inc(S("rot_ready"), 1)
            pool.wait_ge(S("rot_ready"), 2 * t + 2)
            e = slice(NP - 1, T, NS)
            G.tensor_tensor(h_last[:, t, 0], q[:, 0, 0, e], q[:, 1, 1, e], ALU.subtract).then_inc(S("hlast_step"), 1)
            G.tensor_tensor(h_last[:, t, 1], q[:, 0, 1, e], q[:, 1, 0, e], ALU.add).then_inc(S("hlast_step"), 1)
        pool.wait_ge(S("hlast_step"), 2 * ST)
        pool.dma_start(a["h_last"][:], h_last[:]).then_inc(S("h_out"), 16)
        pool.wait_ge(S("h_out"), 16)

    block.__exit__(None, None, None)


INPUTS = ("xT cols w_in par b_raw c_re c_im h0 cacheK cacheV w_glu w_out w_r b_gu b_dn w_gu w_dn "
          "ident ones block_ones tri scan_pat iota mask_p mask_s").split()
OUTPUTS = {"y": (P, KT, T), "new_k": (P, T - P), "new_v": (P, T - P), "roll_k": (P, NB, WIN - NS),
           "roll_v": (WIN - NS, NB, P), "h_last": (P, ST, 2, NB + 1)}


def constants():
    i = np.arange(P)
    q = np.arange(NSAMP)
    f = np.float32
    key_b = np.concatenate([np.repeat(np.arange(NB), WIN), np.repeat(np.arange(NB), NS)])
    key_at = np.concatenate([np.tile(np.arange(WIN), NB), WIN + np.tile(np.arange(NS), NB)])
    row_b, row_s = np.tile(q // NS, 4)[:, None], np.tile(q % NS, 4)[:, None]
    seen = (key_b == row_b) & (key_at > row_s) & (key_at <= row_s + WIN)
    first = np.ones(T, f)
    first[0] = 0
    first[NP::NS] = 0
    out = HD ** 0.5 * NEG
    return {
        "ident": np.eye(P, dtype=f), "ones": np.ones((P, P), f),
        "block_ones": (i[:, None] // HD == i // HD).astype(f), "tri": (i[:, None] < i).astype(f),
        "scan_pat": np.tile(first, (P, 1)), "iota": np.tile(np.arange(SLOTS, dtype=f), (P, 1)),
        "mask_p": np.where(np.concatenate([i > i[:, None], i <= i[:, None]], 1), 0, out).astype(f),
        "mask_s": np.where(seen, 0, out).astype(f),
    }


def columns(v, tiles):
    return v.reshape(tiles, P).T


def layout(x):
    p = np.arange(P)
    heads = np.concatenate([(4 * (p // HD) + i) * HD + p % HD for i in range(4)])
    tokens = np.concatenate([x["x_prompt"].reshape(NP, D), x["x_sample"].reshape(NSAMP, D)])
    w_in = x["w_in"][0]
    att, kv = DS, 2 * HD
    order = np.concatenate([np.arange(att + 2 * kv, att + 2 * kv + DS), heads, np.arange(att, att + 2 * kv)])
    b_glu = x["b_glu"][0]
    sinks = x["attn_sinks"][0]
    lam_re, lam_im = x["ssm_lambda_re"][0], x["ssm_lambda_im"][0]
    log_dt = np.broadcast_to(x["ssm_log_dt"][0][:, None], (NG, SS))

    def parameter(v):
        states = v.reshape(ST, P).T
        rows = np.repeat(v.reshape(CT, 8, SS), SG, axis=1)
        return np.concatenate([states, rows.transpose(1, 0, 2).reshape(P, CT * SS)], 1)

    b_raw = np.zeros((P, 2, CT, 2, SS), np.float32)
    c_mat = np.zeros((2, 2, SS, ST, 2, SG), np.float32)
    for n, (b, c) in enumerate((("ssm_b_re", "ssm_c_re"), ("ssm_b_im", "ssm_c_im"))):
        bb = x[b][0].transpose(0, 2, 1).reshape(CT, 8, SG, SS)
        cc = x[c][0].reshape(ST, 2, SG, SS)
        v = b_raw.reshape(8, SG, 2, CT, 2, SS)
        for g in range(8):
            v[g, :, n, :, g % 2] = bb[:, g].transpose(1, 0, 2)
        for h in range(2):
            c_mat[n, h, :, :, h] = cc[:, h].transpose(2, 0, 1)
    state = np.stack([x["state_ssm_re"][0], x["state_ssm_im"][0]]).reshape(2, NB, ST, P)
    bgu = x["b_gate_up"][0].reshape(NE, KT, P, 2)
    out = {
        "xT": tokens.T.reshape(KT, P, T).transpose(1, 0, 2),
        "cols": np.concatenate([
            columns(x["norm_mix_g"][0], KT), columns(x["norm_ffn_g"][0], KT), np.tile(x["q_norm_g"][0], 2)[:, None],
            np.tile(x["k_norm_g"][0], 2)[:, None], columns(x["attn_out_norm_g"][0][heads], CT),
            columns(x["ssm_out_norm_g"][0], CT), columns(b_glu[:DS], CT), columns(b_glu[DS:], CT),
            columns(x["ssm_d"][0].reshape(-1), CT), np.broadcast_to(sinks, (P, 8)),
            np.repeat(sinks.reshape(2, 4).T, NSAMP, axis=0), np.broadcast_to(x["b_router"][0], (P, NE))], 1),
        "w_in": w_in[:, order].reshape(KT, P, 10, P).transpose(1, 2, 0, 3),
        "par": np.stack([parameter(lam_re), parameter(lam_im), parameter(log_dt)], 1),
        "b_raw": b_raw.reshape(P, 2, CT, P),
        "c_re": c_mat[0].reshape(P, ST, 2 * SG), "c_im": c_mat[1].reshape(P, ST, 2 * SG),
        "h0": state.transpose(3, 2, 0, 1),
        "cacheK": x["cache_k"][0].reshape(NB, WIN, P).transpose(2, 0, 1),
        "cacheV": x["cache_v"][0].reshape(NB, WIN, P).transpose(1, 0, 2),
        "w_glu": x["w_glu"][0].reshape(CT, P, D).transpose(1, 0, 2),
        "w_out": np.concatenate([x["w_out"][0][:DS][heads], x["w_out"][0][DS:]]).reshape(KT, P, D).transpose(1, 0, 2),
        "w_r": x["w_router"][0].reshape(KT, P, NE).transpose(1, 0, 2),
        "b_gu": bgu.transpose(2, 0, 3, 1).reshape(P, NE * 16),
        "b_dn": x["b_down"][0].reshape(NE, KT, P).transpose(2, 0, 1).reshape(P, NE * KT),
        "w_gu": x["w_gate_up"][0].reshape(NE, KT, P, D, 2).transpose(0, 1, 2, 4, 3).reshape(NE, KT, P, 2 * D),
        "w_dn": x["w_down"][0].reshape(NE, 4, 2, P, D).transpose(0, 1, 3, 2, 4),
    }
    return {**out, **constants()}


def kernel(**inputs):
    import concourse.bacc as _bacc
    from concourse.bass_utils import run_bass_kernel_spmd as _run

    nc = _bacc.Bacc("TRN2", target_bir_lowering=False, num_devices=1)
    x = {k: np.asarray(v) for k, v in inputs.items()}
    data = {k: np.ascontiguousarray(v) for k, v in layout(x).items()}
    a = {k: nc.dram_tensor(k + "_dram", data[k].shape, F32, kind="ExternalInput").ap() for k in INPUTS}
    for k, shape in OUTPUTS.items():
        a[k] = nc.dram_tensor(k + "_dram", shape, F32, kind="ExternalOutput").ap()
    build(nc, a)
    got = _run(nc, [{k + "_dram": data[k] for k in INPUTS}], core_ids=[0]).results[0]
    got = {k: np.asarray(got[k + "_dram"]) for k in OUTPUTS}
    y = got["y"].transpose(2, 1, 0).reshape(T, D)
    h = got["h_last"].transpose(2, 3, 1, 0).reshape(2, NB + 1, NG, SS)

    def cache(new, rolled):
        prompt = new[:, 0:WIN].T.reshape(1, 1, WIN, 2, HD)
        fresh = new[:, WIN:].T.reshape(NB, NS, P)
        return prompt, np.concatenate([rolled, fresh], 1).reshape(1, NB, WIN, 2, HD)

    kp, ks = cache(got["new_k"], got["roll_k"].transpose(1, 2, 0))
    vp, vs = cache(got["new_v"], got["roll_v"].transpose(1, 0, 2))
    return (y[:NP].reshape(1, NP, D), y[NP:].reshape(NB, NS, D), kp, vp, h[0, 0][None, None], h[1, 0][None, None],
            ks, vs, h[0, 1:][None], h[1, 1:][None])
```

```python
import numpy as np

import concourse.bass as bass
from concourse import mybir

F32 = mybir.dt.float32
I32 = mybir.dt.int32
U32 = mybir.dt.uint32
ALU = mybir.AluOpType
ACT = mybir.ActivationFunctionType
AX = mybir.AxisListType

P = 128
D = 1024
KT = D // P
NP, NB, NS = 256, 8, 4
NSAMP = NB * NS
T = NP + NSAMP
WIN = 128
DS = 512
CT = DS // P
HD = 64
NG, SG, SS = 32, 16, 64
ST = NG * SS // P
NE, TOPK = 32, 4
SLOTS = 84
FIT = 512 // SLOTS
REPEATS = -(-T // SLOTS) - 1
ITEMS = T * TOPK // SLOTS
PAIRS = NE // 2
EPS = 1e-6
NEG = -1e30
TT = ((0, P), (P, P), (2 * P, T - 2 * P))
NPAR = ST + CT * SS
SAMPLE_KEYS = NB * WIN + NSAMP
TWO_PI = 2 * np.pi
TWO_PI_HI = 6.28125
TWO_PI_LO = float(np.float32(TWO_PI - TWO_PI_HI))
ROUND_MAGIC = 1.5 * 2.0 ** 23
GELU_C = float(np.sqrt(2 / np.pi))

C_GMIX, C_GFFN, C_GQ, C_GK, C_GATT, C_GSSM, C_BA, C_BG, C_D, C_SINK, C_BR = np.cumsum(
    [0, 8, 8, 1, 1, 4, 4, 4, 4, 4, 10]).tolist()
N_COLS = C_BR + NE


def build(nc, a):
    base = nc.sbuf_base
    base += -base % 32
    marks = {"at": base}

    def sb(name, shape, at, dt=F32):
        t = nc.alloc_sbuf_tensor_at(name, [P] + list(shape), dt, offset=base + at)
        return t

    def sz(*shape):
        return int(np.prod(shape)) * 4

    GU, DN = 0, 65536
    REST = 131072
    gu_ring = [sb(f"gu_ring{k}", [2 * D], GU + k * 8192) for k in range(8)]
    dn_ring = [sb(f"dn_ring{k}", [2, D], DN + k * 8192) for k in range(8)]
    w_in = sb("w_in", [10, KT, P], GU)
    pT = sb("pT", [42 * P], GU)
    s_p0 = sb("s_p0", [8, P], GU + 21504)
    s_p1 = sb("s_p1", [8, 2 * P], GU + 25600)
    yT = sb("yT", [CT, T], GU + 33792)
    s_s = sb("s_s", [2, SAMPLE_KEYS], GU + 40960)
    kT = sb("kT", [T], GU + 49408)
    vT = sb("vT", [T], GU + 50560)
    v_tok = sb("v_tok", [3, P], GU + 51712)
    q_rot = [sb(f"q_rot{b}", [2, 2, T], GU + 53248 + b * 4608) for b in range(2)]
    q_s = sb("q_s", [CT * NSAMP], GU + 62464)
    tab_tmp_p = sb("tab_tmp_p", [2, 2, 256], GU + 53248)
    cs = sb("cs", [ST, 2, T], DN)
    w_glu = sb("w_glu", [CT, D], DN + 36864)
    cacheK = sb("cacheK", [NB, WIN], DN + 53248)
    cacheV = sb("cacheV", [NB, P], DN + 57344)
    b_bar = sb("b_bar", [2, CT, P], DN + 61440)
    o = REST
    xT = sb("xT", [KT, T], o); o += 9216
    xg = sb("xg", [KT, T], o)
    mask_p = sb("mask_p", [2 * P], o)
    mask_s = sb("mask_s", [SAMPLE_KEYS], o + 1024); o += 9216
    W16 = o; o += 16384
    w_out = sb("w_out", [CT, D], W16)
    QQ = o
    qT = sb("qT", [CT, T], o); o += 4608
    aT = sb("aT", [CT, T], o)
    ms = sb("ms", [T], o)
    r_mix = sb("r_mix", [T], o + 1152)
    qsq = sb("qsq", [T], o + 2304)
    vv = sb("vv", [T], o + 3456); o += 4608
    xsq = sb("xsq", [KT, T], QQ)
    uT = sb("uT", [CT, T], o); o += 4608
    WK = o
    p1 = sb("p1", [2, T], o); p2 = sb("p2", [2, T], o + 2304)
    v_rot = sb("v_rot", [2, T], o + 4608)
    g_rot = [sb(f"g_rot{b}", [2, T], o + 6912 + b * 2304) for b in range(2)]
    r_scan = [sb(f"r_scan{b}", [2, T], o + 11520 + b * 2304) for b in range(2)]
    b_raw = sb("b_raw", [2, CT, P], WK)
    e_tab = sb("e_tab", [2, ST, 16], GU + 40960)
    f_tab = sb("f_tab", [2, ST, 16], GU + 43008)
    t1 = sb("t1", [2, ST, 16], WK + 8192)
    t2 = sb("t2", [2, ST, 16], WK + 10240)
    tab_tmp = sb("tab_tmp", [2, 2, 256], WK + 8192)
    o += 16128
    ident = sb("ident", [P], o); o += 512
    ones = sb("ones", [P], o); o += 512
    block_ones = sb("block_ones", [P], o); o += 512
    tri = sb("tri", [P], o); o += 512
    scan_pat = sb("scan_pat", [T], o); o += 1152
    iota = sb("iota", [P], o); o += 512
    cT = sb("cT", [3, ST, 32], o); o += 6144
    cols = sb("cols", [N_COLS], o); o += 352
    h0 = sb("h0", [ST, 2, NB], o); o += 1024
    h_last = sb("h_last", [ST, 2, NB + 1], o); o += 1152
    st_mx = sb("st_mx", [24], o); st_neg = sb("st_neg", [18], o + 96)
    st_sum = sb("st_sum", [18], o + 192); st_snk = sb("st_snk", [18], o + 288); o += 384
    mag = sb("mag", [ST], o); o += 64
    flag = sb("flag", [8], o, I32); o += 32
    assert base + o <= nc.sbuf_usable_end, (base + o, nc.sbuf_usable_end)
    par = sb("par", [3, NPAR], W16)
    par_t = [sb(f"par_t{k}", [NPAR], W16 + 3 * sz(NPAR) + k * sz(NPAR)) for k in range(11)]
    bb_tmp = sb("bb_tmp", [2, CT, P], GU + 57344)
    o = W16
    x_tok = [sb(f"x_tok{t}", [D], o + 4096 * t) for t in range(3)]; o += 12288
    xe = sb("xe", [KT, SLOTS], o); o += sz(KT, SLOTS)
    ye_T = sb("ye_T", [KT, SLOTS], o); o += sz(KT, SLOTS)
    YE = o
    ye = sb("ye", [D], o); o += 4096
    grid_e = sb("grid_e", [ITEMS, REPEATS * NE], o)
    grid_r = sb("grid_r", [ITEMS, REPEATS * NE], o + sz(ITEMS, REPEATS * NE))
    hg, hl, th, hT = [sb(n, [KT, SLOTS], o + k * sz(KT, SLOTS)) for k, n in enumerate(("hg", "hl", "th", "hT"))]
    o += max(4 * sz(KT, SLOTS), 2 * sz(ITEMS, REPEATS * NE))
    b_gu = sb("b_gu", [NE * 16], o); o += 2048
    b_dn = sb("b_dn", [NE * 8], o); o += 1024
    oh = sb("oh", [3, P], o); o += sz(3, P)
    goh = sb("goh", [3, SLOTS], o); o += sz(3, SLOTS) + (-sz(3, SLOTS)) % 32
    gT = sb("gT", [T], o); o += 1152
    pos = sb("pos", [3, NE + 2], o); o += 416
    gate = sb("gate", [3, NE + 2], o); o += 416
    sel = sb("sel", [3, NE], o); o += 384
    lg = sb("lg", [3, NE], o); o += 384
    v8 = sb("v8", [3, 8], o); o += 96
    i8 = sb("i8", [3, 8], o, U32); o += 96
    if8 = sb("if8", [3, 8], o); o += 96
    ex4 = sb("ex4", [3, 4], o); o += 64
    gs = sb("gs", [3], o); o += 32
    eq = sb("eq", [3, NE], o); o += 384
    w_r = sb("w_r", [KT, NE], o); o += 1024
    x2sq = sb("x2sq", [2, T], YE)
    r2 = sb("r2", [T], YE + 2304)
    cnt = sb("cnt", [NE], o); o += 128
    entries = sb("entries", [2, REPEATS * NE], o); o += sz(2, REPEATS * NE)
    more = sb("more", [REPEATS * NE], o); o += sz(REPEATS * NE)
    place = sb("place", [REPEATS * NE], o); o += sz(REPEATS * NE)
    one_row = sb("one_row", [REPEATS * NE], o); o += sz(REPEATS * NE)
    list_f = sb("list_f", [16], o); o += 64
    list_shift = sb("list_shift", [16], o); o += 64
    list_e = sb("list_e", [16], o, I32); o += 64
    pos_item = sb("pos_item", [3], o); o += 32
    assert o <= WK + 16128, (o, WK + 16128)

    pb = [nc.alloc_psum_tensor(f"bank{k}", [P, 512], F32) for k in range(8)]
    sems = {}

    def S(name):
        if name not in sems:
            sems[name] = nc.alloc_semaphore(name)
        return sems[name]

    x_in = [S(f"x_in{h}") for h in range(2)]
    wu_in = [S(f"wu_in{c}") for c in range(CT)]
    wq_in = [S(f"wq_in{c}") for c in range(3)]
    for n in ("par_in cols_in b_in const_in c_in h0_in mask_in cacheK_in cacheV_in wglu_in woutA_in woutB_in moe_in "
              "wr_in out_done "
              "xsq_ready xg_ready sum_ready ms_ready ln_done r_mix_ready u_proj u_ready proj_done proj_free "
              "sq_ready qk_sum vv_ready rq_ready raw_ready qk_ready v_ready v_turned v_tok_ready "
              "par_dve par_act bbar_ready bbar_step tab_dve tab_pool tab_act r_scan_ready w_ready w_free g_ready "
              "rot_ready rot_used y_sum y_ready ysq_ready y_poly tanh_ready gelu_ready h0_scaled hlast_step c_neg "
              "score_ready score_used neg_ready exp_done sum_inv p_ready pt_turned pt_ready pv_ready a_part_ready "
              "asq_ready asum_ready qs_ready av_ready ar_ready an_ready outA_done xmid_ready "
              "glu_done ga_ready th_glu s_ready ssq_ready ssum_ready sv_ready sr_ready sn_ready outB_done x2_ready "
              "x2sq_ready x2sum_ready x2v_ready r2_ready xn_ready logits_ready xtok_turned xtok_ready top_ready "
              "exp4_done sel_ready pos_ready route_ready yt_zeroed "
              "oh_ready gathered xe_ready gu_used gu_free hg_ready th_ready h_ready dn_used y_done "
              "goh_ready g_turned gT_ready y_turned ye_ready comb_done acc_done "
              "den_ready den_inv hl_ready hlg_ready goh_step list_ready pos_item_ready h_out "
              "dve_order act_order pool_order result_ready").split():
        S(n)
    gu_in = [S(f"gu_in{k}") for k in range(8)]
    dn_in = [S(f"dn_in{k}") for k in range(8)]
    order = {"dve": 0, "act": 0, "pool": 0}

    def ordered(eng, who, ins):
        order[who] += 1
        ins.then_inc(S(who + "_order"), 1)
        eng.wait_ge(S(who + "_order"), order[who])

    def col(k, n=P):
        return cols[0:n, k:k + 1]

    def wide(ap, axis, n):
        shape = list(ap.shape)
        return ap.unsqueeze(axis).to_broadcast(shape[:axis] + [n] + shape[axis:])

    SCORES = [("p0", 0, 0), ("p0", 1, 0), ("p1", 0, 0), ("p1", 0, 1), ("p1", 1, 0), ("p1", 1, 1),
              ("s", 0, 0), ("s", 0, 1), ("n", 0, 0), ("s", 1, 0), ("s", 1, 1), ("n", 1, 0)]
    TURNS = [("p0", 0, 0), ("p0", 1, 0), ("p1", 0, 0), ("p1", 0, 1), ("p1", 1, 0), ("p1", 1, 1),
             ("s", 0, 0), ("s", 0, 1), ("n", 0, 0), ("s", 1, 0), ("s", 1, 1), ("n", 1, 0)]
    PT_AT, at = [], 0
    for kind, _, _ in TURNS:
        PT_AT.append(at)
        at += 1 if kind == "n" else 4
    assert at == 42
    SCORE_SLOT = {0: range(0, 3), 1: range(3, 6), 2: range(6, 9), 3: range(9, 12)}
    TURN_SLOT = {6: range(0, 4), 7: range(4, 8), 8: range(8, 12)}
    PV_SLOT = 9
    ASUM_SLOT = 10
    OUTA_SLOT = {12: range(0, 2), 13: range(2, 4), 14: range(4, 6), 15: range(6, 8)}
    SLOTS_N = ST + 2

    def load_gu(sp, e, k):
        sp.dma_start(gu_ring[k][:], a["w_gu"][e, k]).then_inc(gu_in[k], 16)

    def load_dn(sp, e, c, j):
        k = 4 * j + c
        sp.dma_start(dn_ring[k][:], a["w_dn"][e, c]).then_inc(dn_in[k], 16)

    def load_first(sp):
        for k in range(8):
            load_gu(sp, 0, k)
        for j in range(2):
            for c in range(4):
                load_dn(sp, j, c, j)

    def load_others(sp):
        def gu(e, e_before, k):
            sp.wait_ge(S("gu_used"), e_before * 8 + (k + 1))
            load_gu(sp, e, k)

        with sp.Fori(0, PAIRS - 1) as i:
            for k in range(8):
                gu(i * 2 + 1, i * 2, k)
            for c in range(4):
                sp.wait_ge(S("dn_used"), i * 8 + (c + 1))
                load_dn(sp, i * 2 + 2, c, 0)
            for k in range(8):
                gu(i * 2 + 2, i * 2 + 1, k)
            for c in range(4):
                sp.wait_ge(S("dn_used"), i * 8 + (4 + c + 1))
                load_dn(sp, i * 2 + 3, c, 1)
        for k in range(8):
            gu(NE - 1, NE - 2, k)

    def pT_sq(c):
        return pT[:, c * T:(c + 1) * T]

    def vsq(c):
        return (p1, p2)[c // 2][:, c % 2]

    def v_glu(x, c):
        return g_rot[c % 2][:, x]

    def gelu_tmp(c):
        return qT[:, c]

    def gelu_square(act, c):
        act.wait_ge(S("y_ready"), c + 1)
        nc.scalar.activation(gelu_tmp(c), yT[:, c], ACT.Square).then_inc(S("ysq_ready"), 1)

    def gelu_tanh(act, c):
        act.wait_ge(S("y_poly"), c + 1)
        nc.scalar.activation(gelu_tmp(c), gelu_tmp(c), ACT.Tanh, scale=GELU_C).then_inc(S("tanh_ready"), 1)

    def table(eng, e, t, tmp, who):
        o1 = tmp[:, 0].rearrange("p x (a b) -> p x a b", a=16)
        o2 = tmp[:, 1].rearrange("p x (a b) -> p x a b", a=16)
        src = wide(e_tab[:, :, t, :], 2, 16)
        eng.tensor_tensor(o1, src, wide(wide(f_tab[:, 0, t, :], 1, 2), 3, 16), ALU.mult)
        ordered(e, who, eng.tensor_tensor(o2, src, wide(wide(f_tab[:, 1, t, :], 1, 2), 3, 16), ALU.mult))
        eng.tensor_tensor(cs[:, t, 0, 0:NP], tmp[:, 0, 0], tmp[:, 1, 1], ALU.subtract)
        return eng.tensor_tensor(cs[:, t, 1, 0:NP], tmp[:, 0, 1], tmp[:, 1, 0], ALU.add)

    block = nc.Block()
    block.__enter__()

    @block.sync
    def _(sp):
        for h in range(2):
            sp.dma_start(xT[:, 4 * h:4 * h + 4, :], a["xT"][:, 4 * h:4 * h + 4, :]).then_inc(x_in[h], 16)
        for c in range(CT):
            sp.dma_start(w_in[:, c], a["w_in"][:, c]).then_inc(wu_in[c], 16)
        for c in range(3):
            sp.dma_start(w_in[:, 4 + 2 * c:6 + 2 * c], a["w_in"][:, 4 + 2 * c:6 + 2 * c]).then_inc(wq_in[c], 16)
        sp.dma_start(cacheK[:], a["cacheK"]).then_inc(S("cacheK_in"), 16)
        sp.dma_start(cacheV[:], a["cacheV"]).then_inc(S("cacheV_in"), 16)
        sp.dma_start(w_glu[:], a["w_glu"]).then_inc(S("wglu_in"), 16)
        sp.wait_ge(S("proj_done"), 6)
        sp.dma_start(mask_p[:], a["mask_p"]).then_inc(S("mask_in"), 16)
        sp.dma_start(mask_s[:], a["mask_s"]).then_inc(S("mask_in"), 16)
        sp.wait_ge(S("bbar_ready"), 1)
        sp.wait_ge(S("h0_scaled"), 1)
        sp.dma_start(w_out[:], a["w_out"][:, 0:CT]).then_inc(S("woutA_in"), 16)
        sp.wait_ge(S("qk_ready"), 5)
        sp.wait_ge(S("v_tok_ready"), 3)
        sp.wait_ge(S("v_ready"), 1)
        sp.dma_start(a["new_k"][:], kT[:, P:T]).then_inc(S("out_done"), 16)
        sp.dma_start(a["new_v"][:], vT[:, P:T]).then_inc(S("out_done"), 16)
        sp.wait_ge(S("cacheK_in"), 16)
        sp.wait_ge(S("cacheV_in"), 16)
        sp.dma_start(a["roll_k"][:], cacheK[:, :, NS:WIN]).then_inc(S("out_done"), 16)
        sp.dma_start(a["roll_v"][:], cacheV[NS:WIN]).then_inc(S("out_done"), 16)
        sp.wait_ge(S("outA_done"), KT)
        sp.dma_start(w_out[:], a["w_out"][:, CT:2 * CT]).then_inc(S("woutB_in"), 16)
        sp.wait_ge(S("glu_done"), 8)
        sp.wait_ge(S("out_done"), 64)
        sp.wait_ge(S("hlast_step"), 2 * ST)
        load_first(sp)
        sp.wait_ge(S("sn_ready"), CT)
        sp.dma_start(w_r[:], a["w_r"]).then_inc(S("wr_in"), 16)
        sp.dma_start(b_gu[:], a["b_gu"]).then_inc(S("moe_in"), 16)
        sp.dma_start(b_dn[:], a["b_dn"]).then_inc(S("moe_in"), 16)
        sp.dma_start(entries[:], a["entries"]).then_inc(S("moe_in"), 16)
        load_others(sp)
        sp.wait_ge(S("list_ready"), 1)
        n = sp.alloc_register("sp_items")
        x_reg = sp.alloc_register("sp_expert")
        sp.reg_load(n, flag[0:1, 0:1])
        with sp.If_cmp(n, 0, "IS_GT"):
            with sp.Fori(0, n) as j:
                sp.reg_load(x_reg, list_e[0:1, bass.ds(j, 1)])
                x = sp.snap(x_reg, min_val=0, max_val=NE - 1)
                for k in range(8):
                    sp.wait_ge(S("gu_used"), j * 8 + (8 * (NE - 1) + k + 1))
                    sp.dma_start(gu_ring[k][:], a["w_gu"][bass.ds(x, 1), k].rearrange("o p f -> (o p) f")).then_inc(
                        gu_in[k], 16)
                for c in range(4):
                    sp.wait_ge(S("dn_used"), j * 4 + (4 * (NE - 1) + c + 1))
                    sp.dma_start(dn_ring[c][:], a["w_dn"][bass.ds(x, 1), c].rearrange("o p k f -> (o p) k f")).then_inc(
                        dn_in[c], 16)
        sp.wait_ge(S("result_ready"), 1)
        sp.dma_start(a["y"][:], xT[:]).then_inc(S("out_done"), 16)
        sp.wait_ge(S("out_done"), 16 * 5)

    @block.tensor
    def _(pe):
        def mm(out, lhsT, rhs, start, stop, **kw):
            return nc.tensor.matmul(out, lhsT, rhs, start=start, stop=stop, **kw)

        pe.wait_ge(S("const_in"), 96)
        for k in range(KT):
            pe.wait_ge(S("xsq_ready"), k + 1)
            last = mm(pb[4][:, 0:T], ones[:], xsq[:, k], k == 0, k == KT - 1)
        last.then_inc(S("sum_ready"), 1)
        pe.wait_ge(S("xg_ready"), KT)
        for c in range(CT):
            pe.wait_ge(wu_in[c], 16)
            for k in range(KT):
                last = mm(pb[c][:, 0:T], w_in[:, c, k], xg[:, k], k == 0, k == KT - 1)
            last.then_inc(S("u_proj"), 1)

        def head_sums(i):
            pe.wait_ge(S("sq_ready"), i + 1)
            if i:
                pe.wait_ge(S("vv_ready"), i)
            mm(pb[7][:, 0:T], block_ones[:], qsq[:], True, True).then_inc(S("qk_sum"), 1)

        for i in range(6):
            pe.wait_ge(wq_in[i // 2], 16)
            if i >= 2:
                pe.wait_ge(S("proj_free"), i - 1)
            for k in range(KT):
                last = mm(pb[5 + i % 2][:, 0:T], w_in[:, 4 + i, k], xg[:, k], k == 0, k == KT - 1)
            last.then_inc(S("proj_done"), 1)
            if i:
                head_sums(i - 1)
        pe.wait_ge(S("v_ready"), 1)
        pe.wait_ge(S("vv_ready"), 5)
        for t, (f, n) in enumerate(TT):
            pe.transpose(pb[7][0:n, t * P:(t + 1) * P], vT[:, f:f + n], ident[:]).then_inc(S("v_turned"), 1)

        def input_product(t):
            c, j = t // 4, t % 4
            if t == 0:
                pe.wait_ge(S("bbar_ready"), 1)
                pe.wait_ge(S("u_ready"), CT)
            if t >= 2:
                pe.wait_ge(S("w_free"), t - 1)
            b = 2 * (t % 2)
            rows = slice(32 * j, 32 * j + 32)
            for x in range(2):
                last = mm(pb[b + x][:, 0:T], b_bar[rows, x, c], uT[rows, c], True, True)
            last.then_inc(S("w_ready"), 1)

        def output_product(t):
            c, j = t // 4, t % 4
            pe.wait_ge(S("rot_ready"), 2 * t + 2)
            if t == 0:
                pe.wait_ge(S("v_tok_ready"), 3)
                pe.wait_ge(S("c_neg"), 2)
            if c >= 2 and j == 0:
                pe.wait_ge(S("y_ready"), c - 1)
            out = pb[4 + 3 * (c % 2)][32 * j:32 * j + 32, 0:T]
            q = q_rot[t % 2]
            for n, (m, x) in enumerate(((0, q[:, 0, 0]), (1, q[:, 1, 1]), (2, q[:, 1, 0]), (2, q[:, 0, 1]))):
                last = mm(out, cT[:, m, t], x, n == 0, n == 3, tile_position=(0, 32 * j))
            last.then_inc(S("rot_used"), 1)

        def score(n):
            kind, kv, part = SCORES[n]
            bank = pb[5 + n % 2]
            if n >= 2:
                pe.wait_ge(S("score_used"), n - 1)
            else:
                pe.wait_ge(S("qk_ready"), 5)
                pe.wait_ge(S("v_ready"), 1)
            rows = slice(HD * kv, HD * kv + HD)
            if kind == "p0":
                for i in range(4):
                    last = mm(bank[:, i * P:(i + 1) * P], qT[rows, i, 0:P], kT[rows, 0:P], True, True)
            elif kind == "p1":
                for i in range(2):
                    last = mm(bank[:, i * 2 * P:(i + 1) * 2 * P], qT[rows, 2 * part + i, P:2 * P], kT[rows, 0:2 * P],
                              True, True)
            elif kind == "s":
                pe.wait_ge(S("qs_ready"), 1)
                pe.wait_ge(S("cacheK_in"), 16)
                last = mm(bank[:], q_s[rows], cacheK[rows, 4 * part:4 * part + 4, :], True, True)
            else:
                last = mm(bank[:, 0:NSAMP], q_s[rows], kT[rows, NP:T], True, True)
            last.then_inc(S("score_ready"), 1)

        def turn(n):
            kind, kv, part = TURNS[n]
            bank = pb[5 + n % 2]
            if n < 2:
                pe.wait_ge(S("score_used"), 12)
            else:
                pe.wait_ge(S("pt_ready"), n - 1)
            pe.wait_ge(S("p_ready"), {"p0": 1, "p1": 2, "s": 3 + kv, "n": 3 + kv}[kind])
            for i in range(1 if kind == "n" else 4):
                if kind == "p0":
                    src = s_p0[:, 4 * kv + i]
                elif kind == "p1":
                    src = s_p1[:, 4 * kv + i, part * P:(part + 1) * P]
                elif kind == "s":
                    src = s_s[:, kv, (4 * part + i) * WIN:(4 * part + i + 1) * WIN]
                else:
                    src = s_s[:, kv, NB * WIN:]
                m = src.shape[1]
                last = pe.transpose(bank[0:m, i * P:(i + 1) * P], src, ident[:])
            last.then_inc(S("pt_turned"), 1)

        def values(n):
            bank = pb[5 + n % 2]
            pe.wait_ge(S("pt_ready"), 12)
            if n == 2:
                pe.wait_ge(S("a_part_ready"), 1)
            for kv in range(2):
                out = bank[HD * kv:HD * kv + HD, :]
                d = slice(HD * kv, HD * kv + HD)
                at = [PT_AT[k] * P for k, u in enumerate(TURNS) if u[1] == kv]
                if n == 0:
                    last = mm(out, v_tok[:, 0, d], pT[:, at[0]:at[0] + 512], True, True, tile_position=(0, HD * kv))
                elif n == 1:
                    for b in range(2):
                        last = mm(out, v_tok[:, b, d], pT[:, at[1 + b]:at[1 + b] + 512], b == 0, b == 1,
                                  tile_position=(0, HD * kv))
                else:
                    pe.wait_ge(S("cacheV_in"), 16)
                    for b in range(NB):
                        f = at[3 + b // 4] + (b % 4) * P
                        mm(out[:, 0:P], cacheV[:, b, d], pT[:, f:f + P], b == 0, False, tile_position=(0, HD * kv))
                    last = mm(out[:, 0:P], v_tok[0:NSAMP, 2, d], pT[0:NSAMP, at[5]:at[5] + P], False, True,
                              tile_position=(0, HD * kv))
            last.then_inc(S("pv_ready"), 1)

        def square_sum(bank, sq, ready, signal):
            for c in range(CT):
                pe.wait_ge(S(ready), c + 1)
                last = mm(pb[bank][:, 0:T], ones[:], sq[c], c == 0, c == CT - 1)
            last.then_inc(S(signal), 1)

        for t in range(SLOTS_N):
            if t < ST:
                input_product(t)
            for n in SCORE_SLOT.get(t, ()):
                score(n)
            for n in TURN_SLOT.get(t, ()):
                turn(n)
            if t == PV_SLOT:
                for n in range(3):
                    values(n)
            if t == ASUM_SLOT:
                pe.wait_ge(S("a_part_ready"), 2)
                square_sum(6, [pT_sq(c) for c in range(CT)], "asq_ready", "asum_ready")
            for m in OUTA_SLOT.get(t, ()):
                if m == 0:
                    pe.wait_ge(S("woutA_in"), 16)
                    pe.wait_ge(S("an_ready"), CT)
                    pe.wait_ge(S("a_part_ready"), 3)
                if m >= 2:
                    pe.wait_ge(S("xmid_ready"), m - 1)
                for k in range(CT):
                    last = mm(pb[5 + m % 2][:, 0:T], w_out[:, k, m * P:(m + 1) * P], aT[:, k], k == 0, k == CT - 1)
                last.then_inc(S("outA_done"), 1)
            if t >= 2:
                output_product(t - 2)
        pe.wait_ge(S("wglu_in"), 16)
        for n in range(2 * CT):
            m = n // 2 + CT * (n % 2)
            if n < 4:
                pe.wait_ge(S("w_free"), ST)
            else:
                pe.wait_ge(S("ga_ready" if n % 2 == 0 else "th_glu"), n // 2 - 1)
            for k in range(CT):
                if n == 0:
                    pe.wait_ge(S("gelu_ready"), k + 1)
                last = mm(pb[n % 4][:, 0:T], w_glu[:, k, m * P:(m + 1) * P], yT[:, k], k == 0, k == CT - 1)
            last.then_inc(S("glu_done"), 1)
        pe.wait_ge(S("y_ready"), CT)
        square_sum(4, [vsq(c) for c in range(CT)], "ssq_ready", "ssum_ready")
        pe.wait_ge(S("sn_ready"), CT)
        pe.wait_ge(S("woutB_in"), 16)
        for m in range(KT):
            if m >= 4:
                pe.wait_ge(S("x2_ready"), m - 3)
            for k in range(CT):
                last = mm(pb[m % 4][:, 0:T], w_out[:, k, m * P:(m + 1) * P], uT[:, k], k == 0, k == CT - 1)
            last.then_inc(S("outB_done"), 1)
        pe.wait_ge(S("sv_ready"), 1)
        for k in range(KT):
            pe.wait_ge(S("x2sq_ready"), k + 1)
            mm(pb[4][:, 0:T], ones[:], x2sq[:, k % 2], k == 0, k == KT - 1).then_inc(S("x2sum_ready"), 1)
        pe.wait_ge(S("wr_in"), 16)
        pe.wait_ge(S("xn_ready"), KT)
        for t, (f, n) in enumerate(TT):
            for k in range(KT):
                last = mm(pb[5][0:n, t * NE:(t + 1) * NE], xg[:, k, f:f + n], w_r[:, k], k == 0, k == KT - 1)
            last.then_inc(S("logits_ready"), 1)
        for u in range(6):
            t, half = u // 2, u % 2
            f, n = TT[t]
            if u == 0:
                pe.wait_ge(S("x2_ready"), KT)
            for k in range(4):
                last = pe.transpose(pb[(0, 1, 2, 3, 6, 7)[u]][0:n, k * P:(k + 1) * P], xg[:, 4 * half + k, f:f + n],
                                    ident[:])
            last.then_inc(S("xtok_turned"), 1)
        pe.wait_ge(S("sel_ready"), 1)
        pe.wait_ge(S("x2v_ready"), 1)
        for t in range(3):
            for s in range(t + 1):
                mm(pb[4][:, t * NE:(t + 1) * NE], ones[:] if s < t else tri[:], sel[:, s], s == 0, s == t)
        for s in range(3):
            last = mm(pb[4][:, 3 * NE:4 * NE], ones[:], sel[:, s], s == 0, s == 2)
        last.then_inc(S("pos_ready"), 1)
        pe.wait_ge(S("xtok_ready"), 6)

        def gather(g):
            pe.wait_ge(S("oh_ready"), g + 1)
            for k in range(KT):
                out = pb[5 + k // 4][:, (k % 4) * P:(k % 4 + 1) * P]
                for t, (f, n) in enumerate(TT):
                    last = mm(out, x_tok[t][0:n, k * P:(k + 1) * P], oh[0:n, t], t == 0, t == 2)
                if k % 4 == 3:
                    last.then_inc(S("gathered"), 1)

        def gate_up(e, g, chunks):
            if chunks[0] == 0:
                pe.wait_ge(S("xe_ready"), g * 2 + 2)
                pe.wait_ge(S("gu_free"), e + 1)
            for k in chunks:
                pe.wait_ge(gu_in[k], e * 16 + 16)
                for m in range(16):
                    last = mm(pb[m // FIT][:, (m % FIT) * SLOTS:(m % FIT + 1) * SLOTS], gu_ring[k][:, m * P:(m + 1) * P],
                              xe[:, k], k == 0 and m % FIT == 0, k == 7, skip_group_check=True)
                last.then_inc(S("gu_used"), 1)

        def down(e, j, fill):
            pe.wait_ge(S("h_ready"), e + 1)
            pe.wait_ge(S("y_done"), e + 1)
            for c in range(4):
                pe.wait_ge(dn_in[4 * j + c], fill * 16)
                for kk in range(2):
                    for m in range(KT):
                        last = mm(pb[3 + m // FIT][:, (m % FIT) * SLOTS:(m % FIT + 1) * SLOTS],
                                  dn_ring[4 * j + c][:, kk, m * P:(m + 1) * P], hT[:, 2 * c + kk],
                                  c == 0 and kk == 0 and m % FIT == 0, c == 3 and kk == 1, skip_group_check=True)
                last.then_inc(S("dn_used"), 1)

        def turn_results(b):
            pe.wait_ge(S("y_done"), b + 1)
            for k in range(KT):
                last = pe.transpose(pb[5 + k // 4][0:SLOTS, (k % 4) * P:(k % 4 + 1) * P], ye_T[:, k], ident[:])
                if k % 4 == 3:
                    last.then_inc(S("y_turned"), 1)
            pe.wait_ge(S("goh_ready"), b + 1)
            for t, (f, n) in enumerate(TT):
                last = pe.transpose(pb[7][0:SLOTS, f:f + n], goh[0:n, t], ident[0:n, 0:n])
            last.then_inc(S("g_turned"), 1)

        def combine(b, xe_wait):
            pe.wait_ge(S("ye_ready"), b * 2 + 2)
            pe.wait_ge(S("gT_ready"), b + 1)
            for m in range(KT):
                if m in (1, 2):
                    pe.wait_ge(S("xe_ready"), xe_wait - (2 - m))
                if m >= 3:
                    pe.wait_ge(S("acc_done"), b * 8 + (m - 2))
                mm(pb[(7, 5, 6)[m % 3]][:, 0:T], ye[0:SLOTS, m * P:(m + 1) * P], gT[0:SLOTS, :], True, True).then_inc(
                    S("comb_done"), 1)

        gather(0)
        with pe.Fori(0, PAIRS) as i:
            for j in range(2):
                e = i * 2 + j
                gate_up(e, e, range(4))
                turn_results(e)
                gate_up(e, e, range(4, 8))
                pe.wait_ge(S("ye_ready"), e * 2 + 2)
                gather(e + 1)
                combine(e, e * 2 + 4)
                down(e, j, i + 1)
        turn_results(NE)
        combine(NE, 2 * NE + 2)
        pe.wait_ge(S("list_ready"), 1)
        n = pe.alloc_register("pe_items")
        pe.reg_load(n, flag[0:1, 0:1])
        with pe.If_cmp(n, 0, "IS_GT"):
            with pe.Fori(0, n) as j:
                pe.wait_ge(S("acc_done"), j * 8 + 8 * (NE + 1))
                gather(j + (NE + 1))
                gate_up(j + NE, j + (NE + 1), range(8))
                down(j + NE, 0, j + (PAIRS + 1))
                turn_results(j + (NE + 1))
                combine(j + (NE + 1), j * 2 + 2 * (NE + 2))

    @block.scalar
    def _(act):
        A = nc.scalar.activation
        for dst, src, s in ((cols, "cols", "cols_in"), (par, "par", "par_in"), (b_raw, "b_raw", "b_in")):
            act.dma_start(dst[:], a[src]).then_inc(S(s), 16)
        for dst, src in ((ident, "ident"), (ones, "ones"), (block_ones, "block_ones"), (tri, "tri"),
                         (scan_pat, "scan_pat"), (iota, "iota")):
            act.dma_start(dst[:], a[src]).then_inc(S("const_in"), 16)
        act.dma_start(h0[:], a["h0"]).then_inc(S("h0_in"), 16)
        act.dma_start(cT[:, 0], a["c_re"]).then_inc(S("c_in"), 16)
        act.dma_start(cT[:, 2], a["c_im"]).then_inc(S("c_in"), 16)
        for k in range(KT):
            act.wait_ge(x_in[k // 4], 16)
            A(xsq[:, k], xT[:, k], ACT.Square).then_inc(S("xsq_ready"), 1)
        act.wait_ge(S("par_in"), 16)
        A(par_t[0][:], par[:, 2], ACT.Exp).then_inc(S("par_act"), 1)
        act.wait_ge(S("par_dve"), 1)
        A(par_t[2][:], par_t[1][:], ACT.Exp).then_inc(S("par_act"), 1)
        act.wait_ge(S("par_dve"), 2)
        A(par_t[5][:], par_t[3][:], ACT.Sin).then_inc(S("par_act"), 1)
        A(par_t[6][:], par_t[4][:], ACT.Sin).then_inc(S("par_act"), 1)

        def rsqrt(dst, src, tmp, waits, signal):
            for s, v in waits:
                act.wait_ge(S(s), v)
            ordered(act, "act", A(tmp, src, ACT.Ln))
            A(dst, tmp, ACT.Exp, scale=-0.5).then_inc(S(signal), 1)

        rsqrt(r_mix[:], ms[:], r_mix[:], [("ms_ready", 1)], "r_mix_ready")
        for i in range(5):
            act.wait_ge(S("proj_done"), i + 1)
            bank = pb[5 + i % 2][:, 0:T]
            if i:
                act.wait_ge(S("qk_sum"), i)
            A(qsq[:], bank, ACT.Square).then_inc(S("sq_ready"), 1)
            A(qT[:, i] if i < 4 else kT[:], bank, ACT.Copy, scale=col(C_GQ if i < 4 else C_GK)).then_inc(
                S("proj_free"), 1)
            if i:
                rsqrt(vv[:], vv[:], vv[:], [("vv_ready", i)], "rq_ready")
        rsqrt(vv[:], vv[:], vv[:], [("vv_ready", 5)], "rq_ready")
        act.wait_ge(S("qk_ready"), 4)
        A(q_s[:].rearrange("p (i q) -> p i q", i=CT), qT[:, :, NP:T], ACT.Copy).then_inc(S("qs_ready"), 1)
        act.wait_ge(S("tab_dve"), 1)
        for x in range(2):
            A(cs[:, :, x, NP:T].rearrange("p t (b s) -> p t b s", b=NB), wide(e_tab[:, x, :, 0:NS], 2, NB),
              ACT.Copy).then_inc(S("tab_act"), 1)

        def scan_factor(t):
            if t >= 2:
                act.wait_ge(S("g_ready"), t - 1)
            A(r_scan[t % 2][:], wide(scan_pat[:], 1, 2), ACT.Copy, scale=mag[:, t:t + 1]).then_inc(
                S("r_scan_ready"), 1)

        def softmax_part(n):
            if n == 0:
                pieces = [(s_p0[:, i], i) for i in range(8)]
            elif n == 1:
                pieces = [(s_p1[:, i], 8 + i) for i in range(8)]
            else:
                pieces = [(s_s[:, n - 2], 14 + n)]
            act.wait_ge(S("neg_ready"), 1)
            for k, (ap, i) in enumerate(pieces):
                last = A(ap, ap, ACT.Exp, bias=st_neg[:, i:i + 1], accum_out=st_sum[:, i:i + 1])
            last.then_inc(S("exp_done"), 1)

        def weights(n):
            if n == 0:
                pieces = [(s_p0[:, i], i) for i in range(8)]
            elif n == 1:
                pieces = [(s_p1[:, i], 8 + i) for i in range(8)]
            else:
                pieces = [(s_s[:, n - 2], 14 + n)]
            act.wait_ge(S("sum_inv"), 1)
            for ap, i in pieces:
                last = A(ap, ap, ACT.Copy, scale=st_sum[:, i:i + 1])
            last.then_inc(S("p_ready"), 1)

        act.wait_ge(S("const_in"), 96)
        act.wait_ge(S("tab_dve"), 2)
        for t in range(SLOTS_N):
            if t < ST:
                scan_factor(t)
            if t == 4:
                act.wait_ge(S("neg_ready"), 1)
                for k in range(4):
                    softmax_part(k)
                A(st_snk[:], st_snk[:], ACT.Exp).then_inc(S("exp_done"), 1)
            if t == 5:
                for k in range(4):
                    weights(k)
            for n in TURN_SLOT.get(t, ()):
                act.wait_ge(S("pt_turned"), n + 1)
                kind = TURNS[n][0]
                rows, width = (NSAMP, P) if kind == "n" else (P, 512)
                A(pT[0:rows, PT_AT[n] * P:PT_AT[n] * P + width], pb[5 + n % 2][0:rows, 0:width], ACT.Copy).then_inc(
                    S("pt_ready"), 1)
            if t == PV_SLOT:
                for n in range(3):
                    act.wait_ge(S("pv_ready"), n + 1)
                    w = P if n < 2 else NSAMP
                    A(aT[:, :, n * P:n * P + w], pb[5 + n % 2][:, 0:4 * w].rearrange("p (i q) -> p i q", i=4),
                      ACT.Copy).then_inc(S("a_part_ready"), 1)
            if t == ASUM_SLOT:
                act.wait_ge(S("a_part_ready"), 3)
                for c in range(CT):
                    A(pT_sq(c), aT[:, c], ACT.Square).then_inc(S("asq_ready"), 1)
                rsqrt(pT[:, 1536:1536 + T], pT[:, 1536:1536 + T], pT[:, 1536:1536 + T], [("av_ready", 1)], "ar_ready")
            if t >= 2 and (t - 2) % 4 == 3:
                gelu_square(act, (t - 2) // 4)
                gelu_tanh(act, (t - 2) // 4)
        act.wait_ge(S("rot_ready"), 2 * ST)
        for c in range(CT):
            act.wait_ge(S("glu_done"), 2 * c + 1)
            if c >= 2:
                act.wait_ge(S("s_ready"), c - 1)
            A(v_glu(0, c), pb[(2 * c) % 4][:, 0:T], ACT.Identity, scale=0.5, bias=col(C_BA + c)).then_inc(S("ga_ready"), 1)
            act.wait_ge(S("glu_done"), 2 * c + 2)
            A(v_glu(1, c), pb[(2 * c + 1) % 4][:, 0:T], ACT.Tanh, scale=0.25, bias=col(C_BG + c)).then_inc(S("th_glu"), 1)
            if c:
                act.wait_ge(S("s_ready"), c)
                A(vsq(c - 1), uT[:, c - 1], ACT.Square).then_inc(S("ssq_ready"), 1)
        act.wait_ge(S("s_ready"), CT)
        A(vsq(CT - 1), uT[:, CT - 1], ACT.Square).then_inc(S("ssq_ready"), 1)
        rsqrt(v_rot[:, 0], v_rot[:, 0], v_rot[:, 0], [("sv_ready", 1)], "sr_ready")
        for k in range(KT):
            act.wait_ge(S("x2_ready"), k + 1)
            if k >= 2:
                act.wait_ge(S("x2sum_ready"), k - 1)
            if k == 0:
                act.wait_ge(S("sn_ready"), CT)
            A(x2sq[:, k % 2], xT[:, k], ACT.Square).then_inc(S("x2sq_ready"), 1)
        rsqrt(r2[:], r2[:], r2[:], [("x2v_ready", 1)], "r2_ready")
        for u in range(6):
            act.wait_ge(S("xtok_turned"), u + 1)
            if u == 0:
                act.wait_ge(S("outB_done"), KT)
            n = TT[u // 2][1]
            A(x_tok[u // 2][0:n, (u % 2) * 512:(u % 2 + 1) * 512], pb[(0, 1, 2, 3, 6, 7)[u]][0:n, :], ACT.Copy).then_inc(
                S("xtok_ready"), 1)
            if u == 3:
                act.wait_ge(S("top_ready"), 1)
                A(ex4[:], ex4[:], ACT.Exp).then_inc(S("exp4_done"), 1)

        def to_experts(g):
            for h in range(2):
                act.wait_ge(S("gathered"), g * 2 + (h + 1))
                A(xe[:, 4 * h:4 * h + 4], pb[5 + h][:].rearrange("p (k s) -> p k s", k=4)[:, :, 0:SLOTS],
                  ACT.Copy).then_inc(S("xe_ready"), 1)

        def act_results(b):
            for h in range(2):
                act.wait_ge(S("y_turned"), b * 2 + (h + 1))
                A(ye[0:SLOTS, 512 * h:512 * h + 512], pb[5 + h][0:SLOTS, :], ACT.Copy).then_inc(S("ye_ready"), 1)
            act.wait_ge(S("g_turned"), b + 2)
            A(gT[0:SLOTS, :], pb[7][0:SLOTS, 0:T], ACT.Copy).then_inc(S("gT_ready"), 1)

        def act_tanh(e):
            act.wait_ge(S("hg_ready"), e + 1)
            A(th[:], hg[:], ACT.Tanh, scale=0.851).then_inc(S("th_ready"), 1)

        to_experts(0)
        with act.Fori(0, PAIRS) as i:
            for j in range(2):
                e = i * 2 + j
                act_results(e)
                act_tanh(e)
                to_experts(e + 1)
        act_results(NE)
        act.wait_ge(S("list_ready"), 1)
        n = act.alloc_register("act_items")
        act.reg_load(n, flag[0:1, 0:1])
        with act.If_cmp(n, 0, "IS_GT"):
            with act.Fori(0, n) as j:
                to_experts(j + (NE + 1))
                act_tanh(j + NE)
                act_results(j + (NE + 1))

    @block.vector
    def _(dve):
        V = nc.vector

        def link(ins):
            ordered(dve, "dve", ins)

        dve.wait_ge(S("cols_in"), 16)
        link(V.tensor_scalar(cols[:, C_BG:C_BG + CT], cols[:, C_BG:C_BG + CT], 0.5, None, ALU.mult))
        for k in range(KT):
            dve.wait_ge(x_in[k // 4], 16)
            V.tensor_scalar(xg[:, k], xT[:, k], col(C_GMIX + k), None, ALU.mult).then_inc(S("xg_ready"), 1)
        dt, lrd, amag, ang, coang, sn, cn, ta, tb, tc, td = [x[:] for x in par_t]
        l_re, l_im = par[:, 0], par[:, 1]
        dve.wait_ge(S("par_in"), 16)
        link(V.tensor_scalar(l_re, l_re, -1e-4, None, ALU.min))
        dve.wait_ge(S("par_act"), 1)
        V.tensor_tensor(lrd, l_re, dt, ALU.mult).then_inc(S("par_dve"), 1)
        link(V.tensor_tensor(ta, l_im, dt, ALU.mult))
        link(V.tensor_scalar(tb, ta, 1 / TWO_PI, ROUND_MAGIC, ALU.mult, ALU.add))
        link(V.tensor_scalar(tb, tb, ROUND_MAGIC, None, ALU.subtract))
        link(V.scalar_tensor_tensor(out=ta, in0=tb, scalar=-TWO_PI_HI, in1=ta, op0=ALU.mult, op1=ALU.add))
        link(V.scalar_tensor_tensor(out=ta, in0=tb, scalar=-TWO_PI_LO, in1=ta, op0=ALU.mult, op1=ALU.add))
        link(V.tensor_scalar(ang, ta, 3.1415925, -3.1415925, ALU.min, ALU.max))
        link(V.tensor_scalar(tb, ang, -1.0, None, ALU.mult))
        link(V.tensor_tensor(tb, tb, ang, ALU.max))
        V.tensor_scalar(coang, tb, -1.0, float(np.pi / 2), ALU.mult, ALU.add).then_inc(S("par_dve"), 1)
        dve.wait_ge(S("sum_ready"), 1)
        V.tensor_scalar(ms[:], pb[4][:, 0:T], 1 / D, EPS, ALU.mult, ALU.add).then_inc(S("ms_ready"), 1)
        dve.wait_ge(S("par_act"), 4)
        V.tensor_copy(mag[:], amag[:, 0:ST])
        V.tensor_copy(e_tab[:, 0, :, 0], cn[:, 0:ST])
        link(V.tensor_copy(e_tab[:, 1, :, 0], sn[:, 0:ST]))

        dve.wait_ge(S("den_ready"), 1)
        V.reciprocal(coang[:, ST:], ang[:, ST:]).then_inc(S("den_inv"), 1)

        def powers(tab, first, m, n, end=False):
            src = tab[:, :, :, first:first + n]
            k = first + m - 1
            o1, o2 = t1[:, :, :, 0:n], t2[:, :, :, 0:n]
            re = wide(wide(tab[:, 0, :, k], 1, 2), 3, n)
            im = wide(wide(tab[:, 1, :, k], 1, 2), 3, n)
            V.tensor_tensor(o1, src, re, ALU.mult)
            link(V.tensor_tensor(o2, src, im, ALU.mult))
            d = slice(first + m, first + m + n)
            V.tensor_tensor(tab[:, 0, :, d], o1[:, 0], o2[:, 1], ALU.subtract)
            last = V.tensor_tensor(tab[:, 1, :, d], o1[:, 1], o2[:, 0], ALU.add)
            if not end:
                link(last)
            return last

        for m in (1, 2, 4, 8):
            powers(e_tab, 0, m, m)
        V.memset(f_tab[:, 0, :, 0], 1.0)
        V.memset(f_tab[:, 1, :, 0], 0.0)
        link(V.tensor_copy(f_tab[:, :, :, 1], e_tab[:, :, :, 15]))
        for m in (1, 2, 4, 8):
            last = powers(f_tab, 1, m, min(m, 15 - m), m == 8)
        last.then_inc(S("tab_dve"), 1)
        dve.wait_ge(S("tab_dve"), 1)
        dve.wait_ge(S("r_mix_ready"), 1)
        for c in range(CT):
            dve.wait_ge(S("u_proj"), c + 1)
            V.tensor_tensor(uT[:, c], pb[c][:, 0:T], r_mix[:], ALU.mult).then_inc(S("u_ready"), 1)
        qk = [0]

        def qk_step():
            i = qk[0]
            qk[0] += 1
            dve.wait_ge(S("qk_sum"), i + 1)
            if i == 0:
                V.tensor_scalar(ms[:], ms[:], EPS * HD, None, ALU.mult).then_inc(S("ms_ready"), 1)
            dve.wait_ge(S("ms_ready"), 2)
            if i:
                dve.wait_ge(S("qk_ready"), i)
            link(V.tensor_tensor(vv[:], pb[7][:, 0:T], ms[:], ALU.add))
            V.tensor_scalar(vv[:], vv[:], 1 / HD, None, ALU.mult).then_inc(S("vv_ready"), 1)
            dve.wait_ge(S("rq_ready"), i + 1)
            dst = qT[:, i] if i < 4 else kT[:]
            V.tensor_tensor(dst, dst, vv[:], ALU.mult).then_inc(S("qk_ready"), 1)

        for t in range(ST // 2):
            last = table(V, dve, t, tab_tmp, "dve")
            if t == ST // 2 - 1:
                last.then_inc(S("tab_dve"), 1)
                dve.wait_ge(S("tab_dve"), 2)
            else:
                link(last)
            if t in (1, 3, 5):
                qk_step()
        qk_step()
        qk_step()
        dve.wait_ge(S("proj_done"), 6)
        V.tensor_tensor(vT[:], pb[6][:, 0:T], r_mix[:], ALU.mult).then_inc(S("v_ready"), 1)
        dve.wait_ge(S("v_turned"), 3)
        for t, (f, n) in enumerate(TT):
            V.tensor_copy(v_tok[0:n, t], pb[7][0:n, t * P:(t + 1) * P]).then_inc(S("v_tok_ready"), 1)

        def ssm_tile(t):
            b = 2 * (t % 2)
            w_re, w_im = pb[b][:, 0:T], pb[b + 1][:, 0:T]
            cos, sin = cs[:, t, 0], cs[:, t, 1]
            if t == 0:
                dve.wait_ge(S("tab_act"), 2)
            if t == ST // 2:
                dve.wait_ge(S("tab_pool"), 1)
            if t == 0:
                dve.wait_ge(S("h0_scaled"), 1)
                dve.wait_ge(S("bbar_ready"), 1)
            dve.wait_ge(S("w_ready"), t + 1)
            V.tensor_tensor(p1[:, 0], w_re, cos, ALU.mult)
            V.tensor_tensor(p1[:, 1], w_im, cos, ALU.mult)
            V.tensor_tensor(p2[:, 0], w_re, sin, ALU.mult)
            V.tensor_tensor(p2[:, 1], w_im, sin, ALU.mult).then_inc(S("w_free"), 1)
            dve.wait_ge(S("w_free"), t + 1)
            V.tensor_tensor(v_rot[:, 0], p1[:, 0], p2[:, 1], ALU.add)
            link(V.tensor_tensor(v_rot[:, 1], p1[:, 1], p2[:, 0], ALU.subtract))
            first = v_rot[:, :, NP:T:NS]
            link(V.tensor_tensor(first, first, h0[:, t], ALU.add))
            dve.wait_ge(S("r_scan_ready"), t + 1)
            if t >= 2:
                dve.wait_ge(S("rot_ready"), 2 * (t - 1))
            V.tensor_tensor_scan(g_rot[t % 2][:].rearrange("p x t -> p (x t)"),
                                 r_scan[t % 2][:].rearrange("p x t -> p (x t)"),
                                 v_rot[:].rearrange("p x t -> p (x t)"), 0.0, ALU.mult, ALU.add).then_inc(S("g_ready"), 1)

        def masked_scores(n):
            kind, kv, part = SCORES[n]
            bank = pb[5 + n % 2]
            dve.wait_ge(S("score_ready"), n + 1)
            if n == 0:
                dve.wait_ge(S("mask_in"), 32)
            sc = HD ** -0.5
            if kind == "p0":
                ops = [(s_p0[:, 4 * kv + i], bank[:, i * P:(i + 1) * P], mask_p[:, P:2 * P], 4 * kv + i) for i in range(4)]
            elif kind == "p1":
                ops = [(s_p1[:, 4 * kv + 2 * part + i], bank[:, i * 2 * P:(i + 1) * 2 * P], mask_p[:],
                        8 + 4 * kv + 2 * part + i) for i in range(2)]
            elif kind == "s":
                f = part * 512
                ops = [(s_s[:, kv, f:f + 512], bank[:], mask_s[:, f:f + 512], 16 + 3 * kv + part)]
            else:
                ops = [(s_s[:, kv, NB * WIN:], bank[:, 0:NSAMP], mask_s[:, NB * WIN:], 18 + 3 * kv)]
            for out, ps, mask, k in ops:
                last = V.tensor_tensor_reduce(out, ps, mask, sc, -3e38, ALU.add, ALU.max, st_mx[:, k:k + 1])
            last.then_inc(S("score_used"), 1)

        def maxima():
            dve.wait_ge(S("score_used"), 12)
            link(V.tensor_reduce(st_mx[:, 22:24], st_mx[:, 16:22].rearrange("p (k j) -> p k j", k=2), AX.X, ALU.max))
            sink8 = cols[:, C_SINK:C_SINK + 8]
            V.tensor_tensor(st_neg[:, 0:8], st_mx[:, 0:8], sink8, ALU.max)
            V.tensor_tensor(st_neg[:, 8:16], st_mx[:, 8:16], sink8, ALU.max)
            link(V.tensor_tensor(st_neg[:, 16:18], st_mx[:, 22:24], cols[:, C_SINK + 8:C_SINK + 10], ALU.max))
            V.tensor_tensor(st_snk[:, 0:8], sink8, st_neg[:, 0:8], ALU.subtract)
            V.tensor_tensor(st_snk[:, 8:16], sink8, st_neg[:, 8:16], ALU.subtract)
            link(V.tensor_tensor(st_snk[:, 16:18], cols[:, C_SINK + 8:C_SINK + 10], st_neg[:, 16:18], ALU.subtract))
            V.tensor_scalar(st_neg[:], st_neg[:], -1.0, None, ALU.mult).then_inc(S("neg_ready"), 1)

        def norm_finish(bank, dst, n, eps, ready, signal):
            dve.wait_ge(S(ready), 1)
            V.tensor_scalar(dst, pb[bank][:, 0:T], 1 / n, eps, ALU.mult, ALU.add).then_inc(S(signal), 1)

        def y_part(c):
            dve.wait_ge(S("rot_used"), 4 * c + 4)
            V.scalar_tensor_tensor(out=yT[:, c], in0=uT[:, c], scalar=col(C_D + c), in1=pb[4 + 3 * (c % 2)][:, 0:T],
                                   op0=ALU.mult, op1=ALU.add).then_inc(S("y_ready"), 1)

        def gelu_poly(c):
            dve.wait_ge(S("ysq_ready"), c + 1)
            link(V.tensor_scalar(gelu_tmp(c), gelu_tmp(c), 0.044715, 1.0, ALU.mult, ALU.add))
            V.tensor_tensor(gelu_tmp(c), gelu_tmp(c), yT[:, c], ALU.mult).then_inc(S("y_poly"), 1)

        def gelu_end(c):
            dve.wait_ge(S("tanh_ready"), c + 1)
            V.scalar_tensor_tensor(out=yT[:, c], in0=gelu_tmp(c), scalar=1.0, in1=yT[:, c], op0=ALU.add,
                                   op1=ALU.mult).then_inc(S("gelu_ready"), 1)

        for t in range(SLOTS_N):
            if t < ST:
                ssm_tile(t)
            for n in SCORE_SLOT.get(t, ()):
                masked_scores(n)
            if t == 3:
                maxima()
            if t == 5:
                dve.wait_ge(S("exp_done"), 5)
                link(V.tensor_tensor(st_sum[:], st_sum[:], st_snk[:], ALU.add))
                V.reciprocal(st_sum[:], st_sum[:]).then_inc(S("sum_inv"), 1)
            if t == ASUM_SLOT:
                norm_finish(6, pT[:, 1536:1536 + T], DS, EPS, "asum_ready", "av_ready")
            if t == ASUM_SLOT + 1:
                dve.wait_ge(S("ar_ready"), 1)
                for c in range(CT):
                    V.scalar_tensor_tensor(out=aT[:, c], in0=aT[:, c], scalar=col(C_GATT + c), in1=pT[:, 1536:1536 + T],
                                           op0=ALU.mult, op1=ALU.mult).then_inc(S("an_ready"), 1)
            for m in OUTA_SLOT.get(t, ()):
                dve.wait_ge(S("outA_done"), m + 1)
                V.tensor_tensor(xT[:, m], xT[:, m], pb[5 + m % 2][:, 0:T], ALU.add).then_inc(S("xmid_ready"), 1)
            if t >= 2 and (t - 2) % 4 == 3:
                c = (t - 2) // 4
                y_part(c)
                gelu_poly(c)
                gelu_end(c)
        for c in range(CT):
            dve.wait_ge(S("ga_ready"), c + 1)
            dve.wait_ge(S("th_glu"), c + 1)
            V.scalar_tensor_tensor(out=uT[:, c], in0=v_glu(1, c), scalar=1.0, in1=v_glu(0, c), op0=ALU.add,
                                   op1=ALU.mult).then_inc(S("s_ready"), 1)
        norm_finish(4, v_rot[:, 0], DS, 4 * EPS, "ssum_ready", "sv_ready")
        dve.wait_ge(S("sr_ready"), 1)
        for c in range(CT):
            V.scalar_tensor_tensor(out=uT[:, c], in0=uT[:, c], scalar=col(C_GSSM + c), in1=v_rot[:, 0],
                                   op0=ALU.mult, op1=ALU.mult).then_inc(S("sn_ready"), 1)
        dve.wait_ge(S("xmid_ready"), KT)
        for m in range(KT):
            dve.wait_ge(S("outB_done"), m + 1)
            V.tensor_tensor(xT[:, m], xT[:, m], pb[m % 4][:, 0:T], ALU.add).then_inc(S("x2_ready"), 1)
        dve.wait_ge(S("x2sum_ready"), KT)
        V.tensor_scalar(r2[:], pb[4][:, 0:T], 1 / D, EPS, ALU.mult, ALU.add).then_inc(S("x2v_ready"), 1)
        V.memset(lg[:], 0.0)
        V.memset(pos[:], -1.0).then_inc(S("gu_free"), 1)
        V.memset(gate[:], 0.0).then_inc(S("g_turned"), 1)
        V.memset(ye_T[:], 0.0).then_inc(S("y_done"), 1)
        dve.wait_ge(S("x2_ready"), KT)
        dve.wait_ge(S("r2_ready"), 1)
        for k in range(KT):
            V.scalar_tensor_tensor(out=xg[:, k], in0=xT[:, k], scalar=col(C_GFFN + k), in1=r2[:],
                                   op0=ALU.mult, op1=ALU.mult).then_inc(S("xn_ready"), 1)
        dve.wait_ge(S("logits_ready"), 3)
        dve.wait_ge(S("y_done"), 1)
        bias = cols[:, C_BR:C_BR + NE]
        V.tensor_tensor(lg[:, 0:2], pb[5][:, 0:2 * NE].rearrange("p (t e) -> p t e", t=2), wide(bias, 1, 2), ALU.add)
        link(V.tensor_tensor(lg[0:NSAMP, 2], pb[5][0:NSAMP, 2 * NE:3 * NE], bias[0:NSAMP], ALU.add))
        for t in range(3):
            last = V.max(v8[:, t], lg[:, t])
        link(last)
        for t in range(3):
            last = V.max_index(i8[:, t], v8[:, t], lg[:, t])
        link(last)
        V.tensor_copy(if8[:], i8[:])
        V.tensor_tensor(ex4[:], v8[:, :, 0:4], wide(v8[:, :, 0], 2, 4), ALU.subtract).then_inc(S("top_ready"), 1)
        iota_e = wide(iota[:, 0:NE], 1, 3)
        dve.wait_ge(S("top_ready"), 1)
        for k in range(TOPK):
            if k == 0:
                link(V.tensor_tensor(sel[:], iota_e, wide(if8[:, :, 0], 2, NE), ALU.is_equal))
            else:
                link(V.tensor_tensor(eq[:], iota_e, wide(if8[:, :, k], 2, NE), ALU.is_equal))
                link(V.tensor_tensor(sel[:], sel[:], eq[:], ALU.add))
        V.tensor_scalar(sel[:, 2], sel[:, 2], tri[:, NSAMP:NSAMP + 1], None, ALU.mult).then_inc(S("sel_ready"), 1)
        dve.wait_ge(S("exp4_done"), 1)
        link(V.tensor_reduce(gs[:], ex4[:], AX.X, ALU.add))
        link(V.reciprocal(gs[:], gs[:]))
        link(V.tensor_tensor(ex4[:], ex4[:], wide(gs[:], 2, 4), ALU.mult))
        G = gate[:, :, 1:1 + NE]
        for k in range(TOPK):
            link(V.tensor_tensor(eq[:], iota_e, wide(if8[:, :, k], 2, NE), ALU.is_equal))
            link(V.tensor_tensor(eq[:], eq[:], wide(ex4[:, :, k], 2, NE), ALU.mult))
            link(V.tensor_tensor(G, G, eq[:], ALU.add))
        dve.wait_ge(S("pos_ready"), 1)
        dve.wait_ge(S("sel_ready"), 1)
        Q = pos[:, :, 1:1 + NE]
        link(V.scalar_tensor_tensor(out=Q, in0=pb[4][:, 0:3 * NE].rearrange("p (t e) -> p t e", t=3), scalar=1.0,
                                    in1=sel[:], op0=ALU.add, op1=ALU.mult))
        V.tensor_scalar(Q, Q, 1.0, None, ALU.subtract)
        link(V.tensor_copy(cnt[:], pb[4][:, 3 * NE:4 * NE]))

        def one_hot(dst, where):
            n = dst.shape[2]
            return V.tensor_tensor(dst[:], wide(iota[:, 0:n], 1, 3), where.to_broadcast((P, 3, n)), ALU.is_equal)

        def build_oh(where, g, first=False):
            if not first:
                dve.wait_ge(S("gathered"), g * 2)
            one_hot(oh, where).then_inc(S("oh_ready"), 1)

        def gated(where, c, b):
            dve.wait_ge(S("g_turned"), b + 1)
            one_hot(goh, where).then_inc(S("goh_step"), 1)
            dve.wait_ge(S("goh_step"), b + 1)
            V.tensor_tensor(goh[:], goh[:], gate[:, :, c].to_broadcast((P, 3, SLOTS)), ALU.mult).then_inc(
                S("goh_ready"), 1)

        def hidden(e, x):
            dve.wait_ge(S("gu_used"), e * 8 + 8)
            for dst, at, first, n in ((hg, 0, 0, FIT), (hg, FIT, FIT, KT - FIT), (hl, 0, KT, 2 * FIT - KT),
                                      (hl, 2 * FIT - KT, 2 * FIT, 2 * KT - 2 * FIT)):
                f = (first % FIT) * SLOTS
                last = V.tensor_tensor(dst[:, at:at + n],
                                       pb[first // FIT][:, f:f + n * SLOTS].rearrange("p (m s) -> p m s", m=n),
                                       wide(b_gu[:, bass.ds(x * 16 + first, n)], 2, SLOTS), ALU.add)
            last.then_inc(S("gu_free"), 1)
            dve.wait_ge(S("gu_free"), e + 2)
            V.tensor_scalar(hg[:], hg[:], 7.0, None, ALU.min).then_inc(S("hg_ready"), 1)
            V.tensor_scalar(hl[:], hl[:], 7.0, -7.0, ALU.min, ALU.max).then_inc(S("hl_ready"), 1)
            dve.wait_ge(S("hl_ready"), e + 1)
            V.scalar_tensor_tensor(out=hl[:], in0=hl[:], scalar=1.0, in1=hg[:], op0=ALU.add, op1=ALU.mult).then_inc(
                S("hlg_ready"), 1)
            dve.wait_ge(S("hlg_ready"), e + 1)
            dve.wait_ge(S("th_ready"), e + 1)
            V.scalar_tensor_tensor(out=hT[:], in0=th[:], scalar=1.0, in1=hl[:], op0=ALU.add, op1=ALU.mult).then_inc(
                S("h_ready"), 1)

        def expert_out(e, x):
            dve.wait_ge(S("dn_used"), e * 4 + 4)
            for first, n in ((0, FIT), (FIT, KT - FIT)):
                last = V.scalar_tensor_tensor(
                    out=ye_T[:, first:first + n], in0=pb[3 + first // FIT][:, 0:n * SLOTS].rearrange("p (m s) -> p m s", m=n),
                    scalar=0.5, in1=wide(b_dn[:, bass.ds(x * 8 + first, n)], 2, SLOTS), op0=ALU.mult, op1=ALU.add)
            last.then_inc(S("y_done"), 1)

        def accumulate(b):
            for m in range(KT):
                dve.wait_ge(S("comb_done"), b * 8 + (m + 1))
                V.tensor_tensor(xT[:, m], xT[:, m], pb[(7, 5, 6)[m % 3]][:, 0:T], ALU.add).then_inc(S("acc_done"), 1)

        def slots_of(c):
            return pos[:, :, bass.ds(c, 1)]

        build_oh(slots_of(1), 0, True)

        dve.wait_ge(S("moe_in"), 48)
        V.memset(one_row[:], 1.0)
        link(V.tensor_tensor(more[:].rearrange("p (r e) -> p r e", r=REPEATS), wide(cnt[:], 1, REPEATS),
                             entries[:, 1].rearrange("p (r e) -> p r e", r=REPEATS), ALU.is_gt))
        link(V.tensor_tensor_scan(place[:], one_row[:], more[:], 0.0, ALU.mult, ALU.add))
        link(V.tensor_copy(flag[:, 0:1], place[:, REPEATS * NE - 1:]))
        link(V.tensor_tensor(place[:], place[:], more[:], ALU.mult))
        link(V.tensor_tensor(grid_e[:], wide(place[:], 1, ITEMS), wide(iota[:, 1:1 + ITEMS], 2, REPEATS * NE), ALU.is_equal))
        link(V.tensor_tensor(grid_r[:], grid_e[:], wide(entries[:, 1], 1, ITEMS), ALU.mult))
        link(V.tensor_tensor(grid_e[:], grid_e[:], wide(entries[:, 0], 1, ITEMS), ALU.mult))
        V.tensor_reduce(list_shift[:, 0:ITEMS], grid_r[:], AX.X, ALU.add)
        link(V.tensor_reduce(list_f[:, 0:ITEMS], grid_e[:], AX.X, ALU.add))
        V.tensor_copy(list_e[:, 0:ITEMS], list_f[:, 0:ITEMS]).then_inc(S("list_ready"), 1)
        dve.wait_ge(S("list_ready"), 1)

        with dve.Fori(0, PAIRS) as i:
            for j in range(2):
                e = i * 2 + j
                gated(slots_of(e), bass.ds(e, 1), e)
                hidden(e, e)
                build_oh(slots_of(e + 2), e + 1)
                accumulate(e)
                expert_out(e, e)
        gated(slots_of(NE), bass.ds(NE, 1), NE)
        accumulate(NE)
        n = dve.alloc_register("dve_items")
        x_reg = dve.alloc_register("dve_expert")
        dve.reg_load(n, flag[0:1, 0:1])
        with dve.If_cmp(n, 0, "IS_GT"):
            with dve.Fori(0, n) as j:
                dve.reg_load(x_reg, list_e[0:1, bass.ds(j, 1)])
                x = dve.snap(x_reg, min_val=0, max_val=NE - 1)
                if_before = pos[:, :, bass.ds(x + 1, 1)].rearrange("p t o -> p (t o)")
                dve.wait_ge(S("acc_done"), j * 8 + 8 * (NE + 1))
                V.tensor_scalar(pos_item[:], if_before, list_shift[:, bass.ds(j, 1)], None, ALU.subtract).then_inc(
                    S("pos_item_ready"), 1)
                dve.wait_ge(S("pos_item_ready"), j + 1)
                build_oh(pos_item[:].unsqueeze(2), j + (NE + 1))
                gated(pos_item[:].unsqueeze(2), bass.ds(x + 1, 1), j + (NE + 1))
                hidden(j + NE, x)
                expert_out(j + NE, x)
                accumulate(j + (NE + 1))
        V.tensor_copy(list_f[:, 1:2], list_f[:, 0:1]).then_inc(S("result_ready"), 1)

    @block.gpsimd
    def _(pool):
        G = nc.gpsimd

        def link(ins):
            ordered(pool, "pool", ins)

        pool.wait_ge(S("c_in"), 32)
        G.tensor_scalar(cT[:, 1], cT[:, 0], -1.0, None, ALU.mult).then_inc(S("c_neg"), 1)
        G.tensor_scalar(cT[:, 2], cT[:, 2], -1.0, None, ALU.mult).then_inc(S("c_neg"), 1)
        lo = ST
        dt, lrd, amag, ang, coang, sn, cn, ta, tb, tc, td = [x[:, lo:] for x in par_t]
        l_re, l_im = par[:, 0, lo:], par[:, 1, lo:]
        pool.wait_ge(S("par_act"), 4)
        pool.wait_ge(S("par_dve"), 2)
        G.tensor_tensor(lrd, amag, cn, ALU.mult)
        G.tensor_tensor(ang, l_re, l_re, ALU.mult)
        link(G.tensor_tensor(tc, amag, sn, ALU.mult))
        G.tensor_tensor(coang, l_im, l_im, ALU.mult)
        link(G.tensor_scalar(lrd, lrd, 1.0, None, ALU.subtract))
        G.tensor_tensor(ang, ang, coang, ALU.add).then_inc(S("den_ready"), 1)
        G.tensor_tensor(ta, lrd, l_re, ALU.mult)
        link(G.tensor_tensor(tb, tc, l_im, ALU.mult))
        link(G.tensor_tensor(ta, ta, tb, ALU.add))
        G.tensor_tensor(tb, tc, l_re, ALU.mult)
        link(G.tensor_tensor(td, lrd, l_im, ALU.mult))
        link(G.tensor_tensor(tb, tb, td, ALU.subtract))
        pool.wait_ge(S("den_inv"), 1)
        G.tensor_tensor(ta, ta, coang, ALU.mult)
        link(G.tensor_tensor(tb, tb, coang, ALU.mult))
        pool.wait_ge(S("b_in"), 16)

        def z(ap):
            return wide(ap.rearrange("p (c s) -> p c s", c=CT), 2, 2)

        def m4(ap):
            return ap.rearrange("p c (h s) -> p c h s", h=2)

        G.tensor_tensor(m4(b_bar[:, 0]), m4(b_raw[:, 0]), z(ta), ALU.mult)
        G.tensor_tensor(m4(bb_tmp[:, 0]), m4(b_raw[:, 1]), z(tb), ALU.mult)
        G.tensor_tensor(m4(b_bar[:, 1]), m4(b_raw[:, 1]), z(ta), ALU.mult)
        link(G.tensor_tensor(m4(bb_tmp[:, 1]), m4(b_raw[:, 0]), z(tb), ALU.mult))
        link(G.tensor_tensor(b_bar[:, 0], b_bar[:, 0], bb_tmp[:, 0], ALU.subtract))
        G.tensor_tensor(b_bar[:, 1], b_bar[:, 1], bb_tmp[:, 1], ALU.add).then_inc(S("bbar_ready"), 1)
        pool.wait_ge(S("bbar_ready"), 1)
        pool.wait_ge(S("h0_in"), 16)
        pool.wait_ge(S("tab_dve"), 1)
        G.tensor_tensor(h0[:], h0[:], wide(wide(mag[:], 2, NB), 2, 2), ALU.mult).then_inc(S("h0_scaled"), 1)
        pool.wait_ge(S("h0_scaled"), 1)
        for t in range(ST // 2, ST):
            last = table(G, pool, t, tab_tmp_p, "pool")
            if t == ST - 1:
                last.then_inc(S("tab_pool"), 1)
                pool.wait_ge(S("tab_pool"), 1)
            else:
                link(last)

        for t in range(ST):
            if t >= 2:
                pool.wait_ge(S("rot_used"), t - 1)
            pool.wait_ge(S("g_ready"), t + 1)
            q = q_rot[t % 2]
            g = g_rot[t % 2]
            for x in range(2):
                G.tensor_tensor(q[:, x], g[:], wide(cs[:, t, x], 1, 2), ALU.mult).then_inc(S("rot_ready"), 1)
            pool.wait_ge(S("rot_ready"), 2 * t + 2)
            e = slice(NP - 1, T, NS)
            G.tensor_tensor(h_last[:, t, 0], q[:, 0, 0, e], q[:, 1, 1, e], ALU.subtract).then_inc(S("hlast_step"), 1)
            G.tensor_tensor(h_last[:, t, 1], q[:, 0, 1, e], q[:, 1, 0, e], ALU.add).then_inc(S("hlast_step"), 1)
        pool.wait_ge(S("hlast_step"), 2 * ST)
        pool.dma_start(a["h_last"][:], h_last[:]).then_inc(S("h_out"), 16)
        pool.wait_ge(S("h_out"), 16)

    block.__exit__(None, None, None)


INPUTS = ("xT cols w_in par b_raw c_re c_im h0 cacheK cacheV w_glu w_out w_r b_gu b_dn w_gu w_dn "
          "ident ones block_ones tri scan_pat iota mask_p mask_s entries").split()
OUTPUTS = {"y": (P, KT, T), "new_k": (P, T - P), "new_v": (P, T - P), "roll_k": (P, NB, WIN - NS),
           "roll_v": (WIN - NS, NB, P), "h_last": (P, ST, 2, NB + 1)}


def constants():
    i = np.arange(P)
    q = np.arange(NSAMP)
    f = np.float32
    key_b = np.concatenate([np.repeat(np.arange(NB), WIN), np.repeat(np.arange(NB), NS)])
    key_at = np.concatenate([np.tile(np.arange(WIN), NB), WIN + np.tile(np.arange(NS), NB)])
    row_b, row_s = np.tile(q // NS, 4)[:, None], np.tile(q % NS, 4)[:, None]
    seen = (key_b == row_b) & (key_at > row_s) & (key_at <= row_s + WIN)
    first = np.ones(T, f)
    first[0] = 0
    first[NP::NS] = 0
    out = HD ** 0.5 * NEG
    return {
        "ident": np.eye(P, dtype=f), "ones": np.ones((P, P), f),
        "block_ones": (i[:, None] // HD == i // HD).astype(f), "tri": (i[:, None] < i).astype(f),
        "scan_pat": np.tile(first, (P, 1)), "iota": np.tile(np.arange(P, dtype=f), (P, 1)),
        "mask_p": np.where(np.concatenate([i > i[:, None], i <= i[:, None]], 1), 0, out).astype(f),
        "entries": np.tile(np.stack([np.tile(np.arange(NE), REPEATS),
                                     np.repeat(SLOTS * np.arange(1, REPEATS + 1), NE)]).astype(f), (P, 1, 1)),
        "mask_s": np.where(seen, 0, out).astype(f),
    }


def columns(v, tiles):
    return v.reshape(tiles, P).T


def layout(x):
    p = np.arange(P)
    heads = np.concatenate([(4 * (p // HD) + i) * HD + p % HD for i in range(4)])
    tokens = np.concatenate([x["x_prompt"].reshape(NP, D), x["x_sample"].reshape(NSAMP, D)])
    w_in = x["w_in"][0]
    att, kv = DS, 2 * HD
    order = np.concatenate([np.arange(att + 2 * kv, att + 2 * kv + DS), heads, np.arange(att, att + 2 * kv)])
    b_glu = x["b_glu"][0]
    sinks = x["attn_sinks"][0]
    lam_re, lam_im = x["ssm_lambda_re"][0], x["ssm_lambda_im"][0]
    log_dt = np.broadcast_to(x["ssm_log_dt"][0][:, None], (NG, SS))

    def parameter(v):
        states = v.reshape(ST, P).T
        rows = np.repeat(v.reshape(CT, 8, SS), SG, axis=1)
        return np.concatenate([states, rows.transpose(1, 0, 2).reshape(P, CT * SS)], 1)

    b_raw = np.zeros((P, 2, CT, 2, SS), np.float32)
    c_mat = np.zeros((2, 2, SS, ST, 2, SG), np.float32)
    for n, (b, c) in enumerate((("ssm_b_re", "ssm_c_re"), ("ssm_b_im", "ssm_c_im"))):
        bb = x[b][0].transpose(0, 2, 1).reshape(CT, 8, SG, SS)
        cc = x[c][0].reshape(ST, 2, SG, SS)
        v = b_raw.reshape(8, SG, 2, CT, 2, SS)
        for g in range(8):
            v[g, :, n, :, g % 2] = bb[:, g].transpose(1, 0, 2)
        for h in range(2):
            c_mat[n, h, :, :, h] = cc[:, h].transpose(2, 0, 1)
    state = np.stack([x["state_ssm_re"][0], x["state_ssm_im"][0]]).reshape(2, NB, ST, P)
    bgu = x["b_gate_up"][0].reshape(NE, KT, P, 2)
    out = {
        "xT": tokens.T.reshape(KT, P, T).transpose(1, 0, 2),
        "cols": np.concatenate([
            columns(x["norm_mix_g"][0], KT), columns(x["norm_ffn_g"][0], KT), np.tile(x["q_norm_g"][0], 2)[:, None],
            np.tile(x["k_norm_g"][0], 2)[:, None], columns(x["attn_out_norm_g"][0][heads], CT),
            columns(x["ssm_out_norm_g"][0], CT), columns(b_glu[:DS], CT), columns(b_glu[DS:], CT),
            columns(x["ssm_d"][0].reshape(-1), CT), np.broadcast_to(sinks, (P, 8)),
            np.repeat(sinks.reshape(2, 4).T, NSAMP, axis=0), np.broadcast_to(x["b_router"][0], (P, NE))], 1),
        "w_in": w_in[:, order].reshape(KT, P, 10, P).transpose(1, 2, 0, 3),
        "par": np.stack([parameter(lam_re), parameter(lam_im), parameter(log_dt)], 1),
        "b_raw": b_raw.reshape(P, 2, CT, P),
        "c_re": c_mat[0].reshape(P, ST, 2 * SG), "c_im": c_mat[1].reshape(P, ST, 2 * SG),
        "h0": state.transpose(3, 2, 0, 1),
        "cacheK": x["cache_k"][0].reshape(NB, WIN, P).transpose(2, 0, 1),
        "cacheV": x["cache_v"][0].reshape(NB, WIN, P).transpose(1, 0, 2),
        "w_glu": x["w_glu"][0].reshape(CT, P, D).transpose(1, 0, 2),
        "w_out": np.concatenate([x["w_out"][0][:DS][heads], x["w_out"][0][DS:]]).reshape(KT, P, D).transpose(1, 0, 2),
        "w_r": x["w_router"][0].reshape(KT, P, NE).transpose(1, 0, 2),
        "b_gu": bgu.transpose(2, 0, 3, 1).reshape(P, NE * 16),
        "b_dn": x["b_down"][0].reshape(NE, KT, P).transpose(2, 0, 1).reshape(P, NE * KT),
        "w_gu": x["w_gate_up"][0].reshape(NE, KT, P, D, 2).transpose(0, 1, 2, 4, 3).reshape(NE, KT, P, 2 * D),
        "w_dn": x["w_down"][0].reshape(NE, 4, 2, P, D).transpose(0, 1, 3, 2, 4),
    }
    return {**out, **constants()}


def kernel(**inputs):
    import concourse.bacc as _bacc
    from concourse.bass_utils import run_bass_kernel_spmd as _run

    nc = _bacc.Bacc("TRN2", target_bir_lowering=False, num_devices=1)
    x = {k: np.asarray(v) for k, v in inputs.items()}
    data = {k: np.ascontiguousarray(v) for k, v in layout(x).items()}
    a = {k: nc.dram_tensor(k + "_dram", data[k].shape, F32, kind="ExternalInput").ap() for k in INPUTS}
    for k, shape in OUTPUTS.items():
        a[k] = nc.dram_tensor(k + "_dram", shape, F32, kind="ExternalOutput").ap()
    build(nc, a)
    got = _run(nc, [{k + "_dram": data[k] for k in INPUTS}], core_ids=[0]).results[0]
    got = {k: np.asarray(got[k + "_dram"]) for k in OUTPUTS}
    y = got["y"].transpose(2, 1, 0).reshape(T, D)
    h = got["h_last"].transpose(2, 3, 1, 0).reshape(2, NB + 1, NG, SS)

    def cache(new, rolled):
        prompt = new[:, 0:WIN].T.reshape(1, 1, WIN, 2, HD)
        fresh = new[:, WIN:].T.reshape(NB, NS, P)
        return prompt, np.concatenate([rolled, fresh], 1).reshape(1, NB, WIN, 2, HD)

    kp, ks = cache(got["new_k"], got["roll_k"].transpose(1, 2, 0))
    vp, vs = cache(got["new_v"], got["roll_v"].transpose(1, 0, 2))
    return (y[:NP].reshape(1, NP, D), y[NP:].reshape(NB, NS, D), kp, vp, h[0, 0][None, None], h[1, 0][None, None],
            ks, vs, h[0, 1:][None], h[1, 1:][None])
```
